# Optimizing a Trainium2 kernel written in Bass

```python
import math
import jax, jax.numpy as jnp
from jax import lax
import numpy as np

D_MODEL = 1024
BATCH = 1
SEQ = 256
DEPTH = 2
DEC_BATCH = 1
DEC_SEQ = 256
PAST_LEN = 128

GRID_W = 64
N_HEADS = 8
N_KV_HEADS = 2
HEAD_DIM = 64
ATTN_W = N_HEADS * HEAD_DIM
KV_W = N_KV_HEADS * HEAD_DIM
ROPE_THETA = 10000.0
Q_BLOCK = 128
POOL_WINDOWS = (2, 4, 8, 16)
POOL_GROUP = 64
POOL_W = POOL_GROUP * len(POOL_WINDOWS)
CONV_W = 256
CONV_K = 31
N_BRANCH = 3
PROJ_W = ATTN_W + 2 * KV_W + POOL_W + 2 * CONV_W + N_BRANCH * D_MODEL
D_FF = 2816
N_EXPERTS = 8
TOP_K = 2
D_FF_EXPERT = 1408
N_DENSE = (DEPTH + 1) // 2
N_MOE = DEPTH // 2
ALPHA = (2 * DEPTH) ** 0.25
BETA = (8 * DEPTH) ** -0.25
LN_EPS = 1e-5
RMS_EPS = 1e-6

kernel_name = "hybrid_gated_encoder_two_batches"

def layer_norm(x, g, b):
    xf = x.astype(jnp.float32)
    mu = jnp.mean(xf, axis=-1, keepdims=True)
    var = jnp.mean(jnp.square(xf - mu), axis=-1, keepdims=True)
    y = (xf - mu) * lax.rsqrt(var + LN_EPS) * g.astype(jnp.float32) + b.astype(jnp.float32)
    return y.astype(x.dtype)

def rms_norm_f32(x, g):
    xf = x.astype(jnp.float32)
    return xf * lax.rsqrt(jnp.mean(xf * xf, axis=-1, keepdims=True) + RMS_EPS) * g.astype(jnp.float32)

def axial_rope_angles(rows):
    row = jnp.repeat(jnp.arange(rows), GRID_W).astype(jnp.float32)
    col = jnp.tile(jnp.arange(GRID_W), rows).astype(jnp.float32)
    n_freq = HEAD_DIM // 4
    inv = ROPE_THETA ** (-jnp.arange(n_freq, dtype=jnp.float32) / n_freq)
    return row[:, None] * inv, col[:, None] * inv

def rope_rotate(x, ang):
    n = ang.shape[-1]
    c = jnp.cos(ang)[:, None, :]
    s = jnp.sin(ang)[:, None, :]
    x1, x2 = x[..., :n], x[..., n:]
    return jnp.concatenate([x1 * c - x2 * s, x2 * c + x1 * s], axis=-1)

def apply_axial_rope(x, ang_row, ang_col):
    half = HEAD_DIM // 2
    return jnp.concatenate([rope_rotate(x[..., :half], ang_row), rope_rotate(x[..., half:], ang_col)], axis=-1)

def gqa_attention(q, k, v):
    b, s, _, _ = q.shape
    g = N_HEADS // N_KV_HEADS
    nb = s // Q_BLOCK
    qb = q.reshape(b, nb, Q_BLOCK, N_KV_HEADS, g, HEAD_DIM).transpose(1, 0, 2, 3, 4, 5)
    scale = HEAD_DIM ** -0.5

    def block(q_blk):
        sc = jnp.einsum('bqkgd,bskd->bkgqs', q_blk, k, preferred_element_type=jnp.float32) * scale
        p = jax.nn.softmax(sc, axis=-1)
        return jnp.einsum('bkgqs,bskd->bqkgd', p.astype(v.dtype), v)

    o = lax.map(block, qb)
    return o.transpose(1, 0, 2, 3, 4, 5).reshape(b, s, ATTN_W)

def multiscale_pool(u):
    b, s, _ = u.shape
    ng = len(POOL_WINDOWS)
    uf = u.astype(jnp.float32).reshape(b, s, ng, POOL_GROUP)
    cs = jnp.concatenate([jnp.zeros((b, 1, ng, POOL_GROUP), jnp.float32), jnp.cumsum(uf, axis=1)], axis=1)
    t = jnp.arange(s)
    outs = []
    for gi, w in enumerate(POOL_WINDOWS):
        lo = w // 2
        hi = w - lo - 1
        start = jnp.clip(t - lo, 0, s)
        end = jnp.clip(t + hi + 1, 0, s)
        csg = cs[:, :, gi]
        tot = jnp.take(csg, end, axis=1) - jnp.take(csg, start, axis=1)
        cnt = (end - start).astype(jnp.float32)[None, :, None]
        outs.append(tot / cnt - uf[:, :, gi])
    return jnp.stack(outs, axis=2)

def conformer_conv(a, gate, w_dw, b_dw, g_ln, b_ln):
    h = a * jax.nn.sigmoid(gate)
    h = lax.conv_general_dilated(h, w_dw[:, None, :].astype(h.dtype), window_strides=(1,),
                                 padding=[(CONV_K // 2, CONV_K // 2)],
                                 dimension_numbers=('NWC', 'WIO', 'NWC'),
                                 feature_group_count=CONV_W) + b_dw
    h = layer_norm(h, g_ln, b_ln)
    return jax.nn.silu(h)

def token_mixer(x, ang_row, ang_col, w_in, b_gate, q_norm_g, k_norm_g, w_attn_out,
                w_pool_mix, pool_scale, w_pool_out, w_dw, b_dw, conv_ln_g, conv_ln_b,
                w_conv_out, w_out):
    b, s, _ = x.shape
    proj = x @ w_in
    o1 = ATTN_W
    o2 = o1 + KV_W
    o3 = o2 + KV_W
    o4 = o3 + POOL_W
    o5 = o4 + CONV_W
    o6 = o5 + CONV_W
    q = proj[..., :o1].reshape(b, s, N_HEADS, HEAD_DIM)
    k = proj[..., o1:o2].reshape(b, s, N_KV_HEADS, HEAD_DIM)
    v = proj[..., o2:o3].reshape(b, s, N_KV_HEADS, HEAD_DIM)
    pool_in = proj[..., o3:o4]
    conv_a = proj[..., o4:o5]
    conv_b = proj[..., o5:o6]
    gates = jax.nn.sigmoid((proj[..., o6:] + b_gate).astype(jnp.float32)).astype(x.dtype)
    gates = gates.reshape(b, s, N_BRANCH, D_MODEL)
    q = apply_axial_rope(rms_norm_f32(q, q_norm_g), ang_row, ang_col).astype(x.dtype)
    k = apply_axial_rope(rms_norm_f32(k, k_norm_g), ang_row, ang_col).astype(x.dtype)
    attn = gqa_attention(q, k, v) @ w_attn_out
    pooled = multiscale_pool(pool_in).astype(x.dtype)
    pool = (jnp.einsum('bsgc,gcd->bsgd', pooled, w_pool_mix).reshape(b, s, POOL_W) * pool_scale) @ w_pool_out
    conv = conformer_conv(conv_a, conv_b, w_dw, b_dw, conv_ln_g, conv_ln_b) @ w_conv_out
    merged = gates[:, :, 0] * attn + gates[:, :, 1] * pool + gates[:, :, 2] * conv
    return merged @ w_out

def swiglu(x, w_g, w_u, w_d):
    return (jax.nn.silu(x @ w_g) * (x @ w_u)) @ w_d

def moe_swiglu(x, w_router, b_router, w_g, w_u, w_d):
    logits = (x @ w_router).astype(jnp.float32) + b_router.astype(jnp.float32)
    top_v, top_i = lax.top_k(logits, TOP_K)
    top_w = jax.nn.softmax(top_v, axis=-1)
    combine = jnp.sum(jax.nn.one_hot(top_i, N_EXPERTS, dtype=jnp.float32) * top_w[..., None], axis=-2)
    combine = combine.astype(x.dtype)
    y = jnp.zeros_like(x)
    for e in range(N_EXPERTS):
        y = y + combine[..., e:e + 1] * swiglu(x, w_g[e], w_u[e], w_d[e])
    return y

def encoder_trunk(x, p):
    s = x.shape[1]
    rows = s // GRID_W
    ang_row, ang_col = axial_rope_angles(rows)
    for l in range(DEPTH):
        mix = token_mixer(x, ang_row, ang_col, p['w_in'][l], p['b_gate'][l], p['q_norm_g'][l], p['k_norm_g'][l],
                          p['w_attn_out'][l], p['w_pool_mix'][l], p['pool_scale'][l], p['w_pool_out'][l],
                          p['w_dw'][l], p['b_dw'][l], p['conv_ln_g'][l], p['conv_ln_b'][l],
                          p['w_conv_out'][l], p['w_out'][l])
        x = layer_norm(ALPHA * x + mix, p['ln1_g'][l], p['ln1_b'][l])
        j = l // 2
        if l % 2 == 0:
            f = swiglu(x, p['w_ff_gate'][j], p['w_ff_up'][j], p['w_ff_down'][j])
        else:
            f = moe_swiglu(x, p['w_router'][j], p['b_router'][j], p['w_e_gate'][j], p['w_e_up'][j], p['w_e_down'][j])
        x = layer_norm(ALPHA * x + f, p['ln2_g'][l], p['ln2_b'][l])
    return x

def setup_inputs(seed: int = 0) -> dict:
    key = jax.random.key(seed)
    ks = jax.random.split(key, 32)
    f32 = jnp.float32

    def nrm(k, shape, scale):
        return jax.random.normal(k, shape, f32) * scale

    def gain(k, shape):
        return 1.0 + 0.02 * jax.random.normal(k, shape, f32)

    return {
        "x_prompt": nrm(ks[0], (BATCH, SEQ, D_MODEL), 1.0),
        "x_sample": nrm(ks[1], (DEC_BATCH, DEC_SEQ, D_MODEL), 1.0),
        "w_in": nrm(ks[2], (DEPTH, D_MODEL, PROJ_W), D_MODEL ** -0.5),
        "b_gate": nrm(ks[3], (DEPTH, N_BRANCH * D_MODEL), 0.02),
        "q_norm_g": gain(ks[4], (DEPTH, HEAD_DIM)),
        "k_norm_g": gain(ks[5], (DEPTH, HEAD_DIM)),
        "w_attn_out": nrm(ks[6], (DEPTH, ATTN_W, D_MODEL), ATTN_W ** -0.5),
        "w_pool_mix": nrm(ks[7], (DEPTH, len(POOL_WINDOWS), POOL_GROUP, POOL_GROUP), POOL_GROUP ** -0.5),
        "pool_scale": gain(ks[8], (DEPTH, POOL_W)),
        "w_pool_out": nrm(ks[9], (DEPTH, POOL_W, D_MODEL), POOL_W ** -0.5),
        "w_dw": nrm(ks[10], (DEPTH, CONV_K, CONV_W), CONV_K ** -0.5),
        "b_dw": nrm(ks[11], (DEPTH, CONV_W), 0.02),
        "conv_ln_g": gain(ks[12], (DEPTH, CONV_W)),
        "conv_ln_b": nrm(ks[13], (DEPTH, CONV_W), 0.02),
        "w_conv_out": nrm(ks[14], (DEPTH, CONV_W, D_MODEL), CONV_W ** -0.5),
        "w_out": nrm(ks[15], (DEPTH, D_MODEL, D_MODEL), BETA * D_MODEL ** -0.5),
        "ln1_g": gain(ks[16], (DEPTH, D_MODEL)),
        "ln1_b": nrm(ks[17], (DEPTH, D_MODEL), 0.02),
        "w_ff_gate": nrm(ks[18], (N_DENSE, D_MODEL, D_FF), D_MODEL ** -0.5),
        "w_ff_up": nrm(ks[19], (N_DENSE, D_MODEL, D_FF), D_MODEL ** -0.5),
        "w_ff_down": nrm(ks[20], (N_DENSE, D_FF, D_MODEL), BETA * D_FF ** -0.5),
        "w_router": nrm(ks[21], (N_MOE, D_MODEL, N_EXPERTS), D_MODEL ** -0.5),
        "b_router": nrm(ks[22], (N_MOE, N_EXPERTS), 0.01),
        "w_e_gate": nrm(ks[23], (N_MOE, N_EXPERTS, D_MODEL, D_FF_EXPERT), D_MODEL ** -0.5),
        "w_e_up": nrm(ks[24], (N_MOE, N_EXPERTS, D_MODEL, D_FF_EXPERT), D_MODEL ** -0.5),
        "w_e_down": nrm(ks[25], (N_MOE, N_EXPERTS, D_FF_EXPERT, D_MODEL), BETA * D_FF_EXPERT ** -0.5),
        "ln2_g": gain(ks[26], (DEPTH, D_MODEL)),
        "ln2_b": nrm(ks[27], (DEPTH, D_MODEL), 0.02),
    }

def reference(x_prompt, x_sample, w_in, b_gate, q_norm_g, k_norm_g, w_attn_out, w_pool_mix, pool_scale,
              w_pool_out, w_dw, b_dw, conv_ln_g, conv_ln_b, w_conv_out, w_out, ln1_g, ln1_b,
              w_ff_gate, w_ff_up, w_ff_down, w_router, b_router, w_e_gate, w_e_up, w_e_down, ln2_g, ln2_b):
    params = dict(w_in=w_in, b_gate=b_gate, q_norm_g=q_norm_g, k_norm_g=k_norm_g, w_attn_out=w_attn_out,
                  w_pool_mix=w_pool_mix, pool_scale=pool_scale, w_pool_out=w_pool_out, w_dw=w_dw, b_dw=b_dw,
                  conv_ln_g=conv_ln_g, conv_ln_b=conv_ln_b, w_conv_out=w_conv_out, w_out=w_out,
                  ln1_g=ln1_g, ln1_b=ln1_b, w_ff_gate=w_ff_gate, w_ff_up=w_ff_up, w_ff_down=w_ff_down,
                  w_router=w_router, b_router=b_router, w_e_gate=w_e_gate, w_e_up=w_e_up, w_e_down=w_e_down,
                  ln2_g=ln2_g, ln2_b=ln2_b)
    y_prompt = encoder_trunk(x_prompt, params)
    y_sample = encoder_trunk(x_sample, params)
    return (y_prompt, y_sample)


_drawn_inputs = setup_inputs


def setup_inputs(seed=0):
    import zlib

    import numpy as np

    out = dict(_drawn_inputs(seed))
    spreads = {}
    factors = {'b_gate': 8.0,
     'q_norm_g': 8.0,
     'k_norm_g': 8.0,
     'pool_scale': 8.0,
     'b_dw': 7.233,
     'conv_ln_g': 8.0,
     'conv_ln_b': 8.0,
     'b_router': 4.256}
    for name, (base, spread) in spreads.items():
        noise = np.random.default_rng([zlib.crc32(name.encode()), seed]).standard_normal(out[name].shape)
        drawn = base * np.exp(spread * noise) if base else spread * noise
        out[name] = __import__('jax').numpy.asarray(drawn.astype(out[name].dtype))
    for name, factor in factors.items():
        out[name] = (out[name] * factor).astype(out[name].dtype)
    return out
```

```python
from contextlib import ExitStack

import numpy as np

import concourse.bass as bass
from concourse import mybir

F32 = mybir.dt.float32
F32R = mybir.dt.float32r
U32 = mybir.dt.uint32
I32 = mybir.dt.int32
ALU = mybir.AluOpType
ACT = mybir.ActivationFunctionType
AX = mybir.AxisListType

P = 128
DEPTH = 2
NB, SEQ = 2, 256
TOK = NB * SEQ
TT = TOK // P
D = 1024
KD = D // P
HD = 64
POOL_WINDOWS = (2, 4, 8, 16)
CK = 31
CPAD = CK // 2
PPAD = 8
FF = 2816
FT = FF // P
NE = 8
FE = 1408
FET = FE // P
ALPHA = (2 * DEPTH) ** 0.25
LN_EPS = 1e-5
RMS_EPS = 1e-6
GRID_W = 64

CH = 1024
N_PROJ, N_BR, N_OUT, N_GU, N_DN = 36, 8, 8, 2 * FT, FT
M_V, M_POOL, M_CA, M_CB, M_GATE = 5, 6, 8, 10, 12
LAYER_BASE = (0, N_PROJ + N_BR + N_OUT + N_GU + N_DN)
N_DENSE = LAYER_BASE[1] + N_PROJ + N_BR + N_OUT
RAW, SPL = 4, 3

CAP = 256
MAX_ITEMS = 11
N_ROWS = (MAX_ITEMS + 1) * CAP
ECH = 2 * FET + KD
DCH = FET * P
ERING = 10
WIDTHS = (64, 96, 128, 160, 192, CAP)

C_ID, C_BLK, C_MEAN, C_ONE, C_TRI = 0, 128, 256, 384, 512
C_COS, C_SIN, C_INV = 640, 896, 1152
C_I8, C_E256, C_I4 = 1664, 1672, 1680
C_END = 1684

V_QG, V_KG, V_BG, V_PS, V_BDW, V_CG, V_CB, V_DW = 0, 1, 2, 26, 28, 30, 32, 34
V_L1G, V_L1B, V_L2G, V_L2B = 96, 104, 112, 120
V_END = 128


def shape_constants():
    c = np.zeros((P, C_END), np.float32)
    c[:, C_ID:C_ID + P] = np.eye(P)
    for h in range(2):
        c[64 * h:64 * h + 64, C_BLK + 64 * h:C_BLK + 64 * h + 64] = 1.0 / HD
    c[:, C_MEAN:C_MEAN + P] = 1.0 / 256
    c[:, C_ONE:C_ONE + P] = 1.0
    c[:, C_TRI:C_TRI + P] = np.triu(np.ones((P, P)), 1)
    nf = HD // 4
    inv = np.float32(10000.0) ** (-np.arange(nf, dtype=np.float32) / np.float32(nf))
    t = np.arange(SEQ)
    for p in range(P):
        half = (p % HD) // 32
        ang = (t // GRID_W if half == 0 else t % GRID_W).astype(np.float32) * inv[p % 16]
        c[p, C_COS:C_COS + SEQ] = np.cos(ang)
        c[p, C_SIN:C_SIN + SEQ] = np.sin(ang) * (-1.0 if p % 32 < 16 else 1.0)
        for ti in range(2):
            w = POOL_WINDOWS[2 * ti + p // 64]
            n = np.clip(t + w - w // 2, 0, SEQ) - np.clip(t - w // 2, 0, SEQ)
            c[p, C_INV + ti * SEQ:C_INV + (ti + 1) * SEQ] = 1.0 / n
    c[:, C_I8:C_I8 + 8] = np.arange(8)
    c[:, C_E256:C_E256 + 8] = np.arange(8) * CAP
    c[:, C_I4:C_I4 + 4] = np.arange(4)
    return c


class Step:

    def __init__(self, eng, sem):
        self.eng, self.sem, self.n, self.base = eng, sem, 0, 0

    def turn(self, base):
        self.base, self.n = base, 0

    def __call__(self, ins):
        self.n += 1
        ins.then_inc(self.sem, 1)
        self.eng.wait_ge(self.sem, self.base + self.n)


def build_trunk(nc, x0, x1, dense_w, expert_gu, expert_dn, consts, vecs, mix, lnrow, wr, br, xd, yd, y0, y1):
    ctx = ExitStack()
    with ctx:
        def sem(name):
            return ctx.enter_context(nc.semaphore(name))

        top = [16512]

        def at(name, shape, dt, offset=None):
            size = 4 * int(np.prod(shape[1:]))
            size = (size + 31) // 32 * 32
            if offset is None:
                offset = top[0]
                top[0] += size
            return nc.alloc_sbuf_tensor_at(name, shape, dt, offset=offset)

        def here():
            return top[0]

        cst = at("cst", [P, C_END], F32)
        vec = at("vec", [P, DEPTH, V_END], F32)
        hvec = at("hvec", [P, DEPTH, 32], F32)
        mixw = at("mixw", [P, DEPTH, 2, P], F32)
        eps = at("eps", [P, 2], F32)
        wrt = at("wrt", [P, KD, NE], F32)
        brt = at("brt", [P, NE], F32)
        stats = at("stats", [P, TT, 2, 6], F32)
        mv = at("mv", [P, TT, 2], F32)
        rstd = at("rstd", [P, TT], F32)
        smx = at("smx", [P, 4, 4], F32)
        lngb = at("lngb", [P, 2, D], F32)
        X = at("X", [P, TT, D], F32)
        o_xth = here()
        xth = at("xth", [P, KD, TOK], F32R)
        xt32 = at("xt32", [P, KD, TOK], F32, o_xth)
        xtl = at("xtl", [P, KD, TOK], F32R)
        raw = at("raw", [P, RAW, CH], F32)
        whi = at("whi", [P, SPL, CH], F32R)
        wlo = at("wlo", [P, SPL, CH], F32R)
        o_m = here()
        gates = at("gates", [P, 24, TOK], F32)
        o = o_m + 10 * 2048
        rms = at("rms", [P, 2, TOK], F32, o)
        shuf = at("shuf", [P, 1, TOK], F32, o + 4096)
        sq = at("sq", [P, 2, TOK], F32, o + 6144)
        o = o_m + 15 * 2048
        PW = SEQ + 2 * PPAD
        upad = at("upad", [P, 2, NB, PW], F32, o)
        psa = at("psa", [P, 2, NB, PW], F32, o + 16 * PW)
        psb = at("psb", [P, 2, NB, PW], F32, o + 32 * PW)
        pooled = at("pooled", [P, 2, TOK], F32, o + 48 * PW)
        assert o + 48 * PW + 4096 <= here()
        o_q = here()
        qk = at("qk", [P, 5, TOK], F32)
        atth = at("atth", [P, 4, TOK], F32R, o_q)
        o_s = here()
        prob = at("prob", [P, 4, SEQ], F32)
        probt = at("probt", [P, 2, 2, SEQ], F32)
        vt = at("vt", [P, TOK], F32)
        vtok = at("vtok", [P, TT, P], F32)
        glu = at("glu", [P, 2, TOK], F32, o_s)
        csq = at("csq", [P, 2, TOK], F32, o_s)
        crs = at("crs", [P, 2, TOK], F32, o_s + 4096)
        mrg = at("mrg", [P, 2, 3, TOK], F32, o_s)
        o_al = here()
        att32 = at("att32", [P, 4, TOK], F32)
        attl = at("attl", [P, 4, TOK], F32R, o_al)
        o_pl = here()
        pm32 = at("pm32", [P, 2, TOK], F32)
        pml = at("pml", [P, 2, TOK], F32R, o_pl)
        pmh = at("pmh", [P, 2, TOK], F32R)
        CW = SEQ + 2 * CPAD
        hpad = at("hpad", [P, 2, NB, CW], F32)
        o_cl = here()
        cv = at("cv", [P, 2, TOK], F32)
        cvl = at("cvl", [P, 2, TOK], F32R, o_cl)
        cvh = at("cvh", [P, 2, TOK], F32R)
        assert here() <= nc.sbuf_usable_end, here()
        xs = at("xs", [P, 2, TOK], F32, o_s)
        hh = at("hh", [P, FT, TOK], F32R, o_m)
        hl = at("hl", [P, FT, TOK], F32R, o_m + FT * 2048)
        fb = at("fb", [P, 3, TOK], F32, o_m + 2 * FT * 2048)
        assert o_m + 2 * FT * 2048 + 6144 <= here()
        top[0] = o_m
        ring = at("ring", [P, ERING, DCH], F32)
        lg = at("lg", [P, TT, NE], F32)
        mx8 = at("mx8", [P, TT, NE], F32)
        ix8 = at("ix8", [P, TT, NE], U32)
        ixf = at("ixf", [P, TT, NE], F32)
        pick = at("pick", [P, 2, TT, NE], F32)
        both = at("both", [P, TT, NE], F32)
        mixk = at("mixk", [P, 2, TT], F32)
        etmp = at("etmp", [P, 4, TT], F32)
        pos = at("pos", [P, TT, NE], F32)
        cnt = at("cnt", [P, NE], F32)
        small = at("small", [P, 8, NE], F32)
        row = at("row", [P, TT, NE], F32)
        rtmp = at("rtmp", [P, TT, NE], F32)
        rowk = at("rowk", [P, 2, TT], F32)
        ridx = at("ridx", [P, 2, TT], U32)
        tabf = at("tabf", [P, 32], F32)
        tab = at("tab", [P, 32], I32)
        t48 = at("t48", [P, 4, NE], F32)
        wcls = at("wcls", [P, 2, MAX_ITEMS + 1], F32)
        assert here() <= nc.sbuf_usable_end
        top[0] = o_xth + KD * TOK * 4
        rows = at("rows", [P, 2, D], F32)
        xg = at("xg", [P, KD, CAP], F32)
        eh = at("eh", [P, FET, CAP], F32)
        eb = at("eb", [P, 3, CAP], F32)
        assert here() <= o_m, (here(), o_m)
        yt = at("yt", [P, KD, CAP], F32, o_xth)
        yrows = at("yrows", [P, 2, D], F32, o_xth + 8192)
        yg = at("yg", [P, 2, TT, D], F32, o_m)
        zero = at("zero", [P, 2048], F32, o_al)

        bank = [ctx.enter_context(nc.psum_tensor(f"bank{i}", [P, 512], F32)) for i in range(8)]

        in_x = sem("in_x")
        in_small = sem("in_small")
        in_ln = sem("in_ln")
        in_ring = [sem(f"in_raw{i}") for i in range(RAW)]
        hi_done, lo_done, pe_chunk = sem("hi_done"), sem("lo_done"), sem("pe_chunk")
        act_step, dve_step, pool_step = sem("act_step"), sem("dve_step"), sem("pool_step")
        setup_done = sem("setup_done")
        ln_mv, ln_sd, ln_norm = sem("ln_mv"), sem("ln_sd"), sem("ln_norm")
        xt_tr, xs_full, xt_hi, xt_lo = sem("xt_tr"), sem("xs_full"), sem("xt_hi"), sem("xt_lo")
        x_affine = sem("x_affine")
        proj_evac = sem("proj_evac")
        rms_ms, rms_sd, roped = sem("rms_ms"), sem("rms_sd"), sem("roped")
        v_tr, v_tok = sem("v_tr"), sem("v_tok")
        pads = sem("pads")
        pool_in, pool_mm, pool_mixed, pool_hi, pool_lo = (sem("pool_in"), sem("pool_mm"), sem("pool_mixed"),
                                                         sem("pool_hi"), sem("pool_lo"))
        glu_th, conv_done, conv_mean, conv_cent = sem("glu_th"), sem("conv_done"), sem("conv_mean"), sem("conv_cent")
        conv_sq, conv_var, conv_sd, conv_nrm, conv_z, conv_act, conv_hi, conv_lo = (
            sem("conv_sq"), sem("conv_var"), sem("conv_sd"), sem("conv_nrm"), sem("conv_z"), sem("conv_act"),
            sem("conv_hi"), sem("conv_lo"))
        sc_mm, sc_max, sc_exp, sc_norm = sem("sc_mm"), sem("sc_max"), sem("sc_exp"), sem("sc_norm")
        p_tr, p_ta, p_tb = sem("p_tr"), sem("p_ta"), sem("p_tb")
        pv_mm, att_full, att_hi, att_lo = sem("pv_mm"), sem("att_full"), sem("att_hi"), sem("att_lo")
        br_gated, br_sum, mg_hi, mg_lo = sem("br_gated"), sem("br_sum"), sem("mg_hi"), sem("mg_lo")
        z_done = sem("z_done")
        ff_th, ff_h, ff_hi, ff_lo = sem("ff_th"), sem("ff_h"), sem("ff_hi"), sem("ff_lo")
        xt_full = sem("xt_full")
        zeroed, rt_logit, rt_both, rt_cnt, rt_e, rt_tab = (sem("zeroed"), sem("rt_logit"), sem("rt_both"),
                                                          sem("rt_cnt"), sem("rt_e"), sem("rt_tab"))
        rt_d = sem("rt_d")
        rt_mix = sem("rt_mix")
        zero_set = sem("zero_set")
        scattered = sem("scattered")
        rows_in, rows_tr, xg_a, xg_b = sem("rows_in"), sem("rows_tr"), sem("xg_a"), sem("xg_b")
        in_e = [sem(f"in_e{i}") for i in range(ERING)]
        e_used = sem("e_used")
        e_th, e_h, e_yt, e_ytr, e_yr, e_out = (sem("e_th"), sem("e_h"), sem("e_yt"), sem("e_ytr"), sem("e_yr"),
                                               sem("e_out"))
        all_stored = sem("all_stored")
        gathered = sem("gathered")
        out_done = sem("out_done")
        y_ready = sem("y_ready")

        ident = cst[:, C_ID:C_ID + P]
        cos2 = cst[:, C_COS:C_COS + SEQ].unsqueeze(1).broadcast_to([P, NB, SEQ])
        sin2 = cst[:, C_SIN:C_SIN + SEQ].unsqueeze(1).broadcast_to([P, NB, SEQ])

        def halves(ap):
            return ap.rearrange("p (b t) -> p b t", b=NB)

        def vcol(layer, c):
            return vec[:, layer, c:c + 1]

        n_xt = [8 * i for i in range(5)]

        def out_bank(c, tt, per):
            if per == N_OUT // 2:
                return (6, 7, 0, 1, 2, 3, 4, 5)[TT * c + tt]
            return (4, 5, 6, 7, 0, 1, 2, 3)[TT * c + tt]


        block = ctx.enter_context(nc.Block())

        @block.sync
        def _(sp):
            for b, src in ((0, x0), (1, x1)):
                sp.dma_start(X[:, 2 * b:2 * b + 2, :], src.rearrange("o (t p) d -> p (o t) d", p=P)).then_inc(in_x, 16)
            sp.dma_start(cst[:, :], consts).then_inc(in_small, 16)
            sp.dma_start(vec[:, :, :], vecs).then_inc(in_small, 16)
            sp.dma_start(mixw[:, :, :, :], mix).then_inc(in_small, 16)
            sp.dma_start(wrt[:, :, :], wr.rearrange("o (k p) e -> p (o k) e", p=P)).then_inc(in_small, 16)
            sp.dma_start(brt[:, :], br.broadcast_to([P, NE])).then_inc(in_small, 16)

            def ln_rows(n):
                if n > 0:
                    sp.wait_ge(x_affine, TT * n)
                sp.dma_start(lngb[:, :, :], lnrow[n:n + 1].broadcast_to([P, 2, D])).then_inc(in_ln, 16)

            ln_at = {LAYER_BASE[0] + 40: 0, LAYER_BASE[0] + 100: 1, LAYER_BASE[1] + 40: 2}
            for g in range(N_DENSE):
                if g >= RAW:
                    sp.wait_ge(lo_done, g - RAW + 1)
                sp.dma_start(raw[:, g % RAW, :], dense_w[g]).then_inc(in_ring[g % RAW], 16)
                if g in ln_at:
                    ln_rows(ln_at[g])
            sp.wait_ge(mg_lo, 2 * KD)

            def expert_chunk(e, k):
                if k < 2 * FET:
                    src = expert_gu[bass.ds(e * (2 * FET) + k, 1)].rearrange("o p n -> (o p) n")
                    dst = ring[:, k % ERING, 0:CH]
                else:
                    src = expert_dn[bass.ds(e * KD + (k - 2 * FET), 1)].rearrange("o p n -> (o p) n")
                    dst = ring[:, k % ERING, 0:DCH]
                sp.dma_start(dst, src).then_inc(in_e[k % ERING], 16)

            for k in range(ECH):
                if k >= ERING:
                    sp.wait_ge(e_used, k - ERING + 1)
                expert_chunk(0, k)
                if k == ERING - 1:
                    ln_rows(3)
            sp.wait_ge(rt_tab, 1)
            turns = sp.value_load(tab[0:1, 24:25], min_val=NE, max_val=MAX_ITEMS)
            with sp.Fori(1, turns) as j:
                e = sp.value_load(tab[0:1, bass.ds(j, 1)], min_val=0, max_val=NE - 1)
                for k in range(ECH):
                    sp.wait_ge(e_used, j * ECH + (k - ERING + 1))
                    expert_chunk(e, k)
            sp.wait_ge(y_ready, 2)
            sp.dma_start(y0.rearrange("o (t p) d -> p (o t) d", p=P), X[:, 0:2, :]).then_inc(out_done, 16)
            sp.wait_ge(y_ready, 4)
            sp.dma_start(y1.rearrange("o (t p) d -> p (o t) d", p=P), X[:, 2:4, :]).then_inc(out_done, 16)
            sp.wait_ge(out_done, 32)

        @block.scalar
        def _(act):
            step = Step(act, act_step)

            def split(g):
                if g >= N_DENSE:
                    return
                act.wait_ge(in_ring[g % RAW], 16 * (g // RAW + 1))
                if g >= SPL:
                    act.wait_ge(pe_chunk, g - SPL + 1)
                nc.scalar.activation(whi[:, g % SPL, :], raw[:, g % RAW, :], ACT.Copy).then_inc(hi_done, 1)

            def ln_sqrt(n):
                for tt in range(TT):
                    act.wait_ge(ln_mv, TT * n + tt + 1)
                    nc.scalar.activation(rstd[:, tt:tt + 1], mv[:, tt, 1:2], ACT.Sqrt,
                                         bias=eps[:, 0:1]).then_inc(ln_sd, 1)

            def xt_evac(n, layer, gcol, bcol):
                for k in range(KD):
                    act.wait_ge(xt_tr, n_xt[n] + k + 1)
                    if n == 3:
                        nc.scalar.activation(xt32[:, k, :], bank[k][:, :], ACT.Identity, scale=vcol(layer, gcol + k),
                                             bias=vcol(layer, bcol + k)).then_inc(xt_full, 1)
                        continue
                    if k >= 2:
                        act.wait_ge(xt_lo, n_xt[n] + k - 1)
                    if n == 0:
                        nc.scalar.activation(xs[:, k % 2, :], bank[k][:, :], ACT.Copy).then_inc(xs_full, 1)
                    else:
                        nc.scalar.activation(xs[:, k % 2, :], bank[k][:, :], ACT.Identity, scale=vcol(layer, gcol + k),
                                             bias=vcol(layer, bcol + k)).then_inc(xs_full, 1)
                    act.wait_ge(xs_full, n_xt[n] + k + 1)
                    nc.scalar.activation(xth[:, k, :], xs[:, k % 2, :], ACT.Copy).then_inc(xt_hi, 1)

            def proj_out(L, m):
                act.wait_ge(pe_chunk, LAYER_BASE[L] + m + 1)
                src = bank[m % 3]
                if m <= 4:
                    nc.scalar.activation(qk[:, m, :], src[:, :], ACT.Copy)
                    if m >= 2:
                        act.wait_ge(rms_ms, 5 * L + m - 1)
                    last = nc.scalar.activation(sq[:, m % 2, :], src[:, :], ACT.Square)
                elif m == M_V:
                    last = nc.scalar.activation(vt[:, :], src[:, :], ACT.Copy)
                elif m < M_CA:
                    act.wait_ge(pads, L + 1)
                    last = nc.scalar.activation(upad[:, m - M_POOL, :, PPAD:PPAD + SEQ], halves(src[:, :]), ACT.Copy)
                elif m < M_CB:
                    last = nc.scalar.activation(hpad[:, m - M_CA, :, CPAD:CPAD + SEQ], halves(src[:, :]), ACT.Copy,
                                                scale=0.5)
                elif m < M_GATE:
                    last = nc.scalar.activation(glu[:, m - M_CB, :], src[:, :], ACT.Tanh, scale=0.5)
                else:
                    last = nc.scalar.activation(gates[:, m - M_GATE, :], src[:, :], ACT.Tanh, scale=0.5,
                                                bias=hvec[:, L, m - M_GATE:m - M_GATE + 1])
                last.then_inc(proj_evac, 1)

            def side(L, m):
                if 2 <= m <= 6:
                    i = m - 2
                    act.wait_ge(rms_ms, 5 * L + i + 1)
                    if i >= 2:
                        act.wait_ge(roped, 5 * L + i - 1)
                    nc.scalar.activation(rms[:, i % 2, :], bank[3 + i % 2][:, :], ACT.Sqrt,
                                         bias=eps[:, 1:2]).then_inc(rms_sd, 1)
                if m == 8:
                    act.wait_ge(v_tr, L + 1)
                    nc.scalar.activation(vtok[:, :, :], bank[5][:, :].rearrange("p (t n) -> p t n", t=TT),
                                         ACT.Copy).then_inc(v_tok, 1)
                s = m - M_GATE
                if s == 2:
                    for ti in range(2):
                        act.wait_ge(pool_mm, 2 * L + ti + 1)
                        step(nc.scalar.activation(pm32[:, ti, :], bank[5 + ti][:, :], ACT.Copy,
                                                  scale=hvec[:, L, 24 + ti:25 + ti]))
                        nc.scalar.activation(pmh[:, ti, :], pm32[:, ti, :], ACT.Copy).then_inc(pool_hi, 1)
                if s >= 1 and s % 2 == 1 and s // 2 < 8:
                    u = s // 2
                    act.wait_ge(sc_max, 8 * L + u + 1)
                    if u >= 1:
                        act.wait_ge(p_tr, 8 * L + u)
                    for q in range(4):
                        a, qt = q // 2, q % 2
                        last = nc.scalar.activation(prob[:, q, :], bank[3 + a][:, qt * SEQ:(qt + 1) * SEQ], ACT.Exp,
                                                    bias=smx[:, 1, q:q + 1], scale=HD ** -0.5,
                                                    accum_out=smx[:, 2, q:q + 1])
                    last.then_inc(sc_exp, 1)
                if s >= 3 and s % 2 == 1 and s // 2 - 1 < 8:
                    u = s // 2 - 1
                    act.wait_ge(p_tr, 8 * L + u + 1)
                    if u >= 1:
                        act.wait_ge(pv_mm, 8 * L + u)
                    nc.scalar.activation(probt[:, 0], bank[5][:, :].rearrange("p (s q) -> p s q", s=2),
                                         ACT.Copy).then_inc(p_ta, 1)
                if s >= 4 and s % 2 == 0 and s // 2 - 2 < 8:
                    u = s // 2 - 2
                    b, mt = u // 4, u % 4
                    act.wait_ge(pv_mm, 8 * L + u + 1)
                    cols = slice(b * SEQ, (b + 1) * SEQ)
                    if L == 0 and u == 0:
                        act.wait_ge(e_out, 16)
                    nc.scalar.activation(att32[:, mt, cols], bank[7][:, 0:SEQ], ACT.Copy,
                                         scale=0.5).then_inc(att_full, 1)
                    act.wait_ge(att_full, 8 * L + u + 1)
                    nc.scalar.activation(atth[:, mt, cols], att32[:, mt, cols], ACT.Copy).then_inc(att_hi, 1)
                if s == 19:
                    act.wait_ge(conv_cent, 2 * L + 2)
                    for ti in range(2):
                        last = nc.scalar.activation(csq[:, ti, :], cv[:, ti, :], ACT.Square)
                    last.then_inc(conv_sq, 1)
                if s == 21:
                    act.wait_ge(conv_var, L + 1)
                    nc.scalar.activation(crs[:, 0, :], bank[4][:, :], ACT.Sqrt, bias=eps[:, 0:1]).then_inc(conv_sd, 1)
                if s == 22:
                    for ti in range(2):
                        act.wait_ge(conv_nrm, 2 * L + ti + 1)
                        step(nc.scalar.activation(cv[:, ti, :], cv[:, ti, :], ACT.Identity,
                                                  scale=hvec[:, L, 26 + ti:27 + ti], bias=hvec[:, L, 28 + ti:29 + ti]))
                        nc.scalar.activation(csq[:, ti, :], cv[:, ti, :], ACT.Tanh, scale=2.0).then_inc(conv_z, 1)
                if s == 23:
                    for ti in range(2):
                        act.wait_ge(conv_act, 2 * L + ti + 1)
                        nc.scalar.activation(cvh[:, ti, :], cv[:, ti, :], ACT.Copy).then_inc(conv_hi, 1)

            act.wait_ge(zero_set, 1)
            act.dma_start(yd[NE * CAP:(NE + 1) * CAP].rearrange("(p s) d -> p (s d)", p=P), zero[:, :]).then_inc(e_out, 16)
            act.wait_ge(in_small, 80)
            act.wait_ge(setup_done, 1)
            xt_evac(0, 0, 0, 0)
            split(0)
            split(1)
            for L in range(DEPTH):
                base = LAYER_BASE[L]
                for m in range(N_PROJ):
                    split(base + m + 2)
                    side(L, m)
                    proj_out(L, m)
                for j in range(N_BR):
                    split(base + N_PROJ + j + 2)
                    act.wait_ge(br_sum, KD * L + j + 1)
                    nc.scalar.activation(xth[:, j, :], mrg[:, j % 2, 0, :], ACT.Copy).then_inc(mg_hi, 1)
                for j in range(N_OUT):
                    split(base + N_PROJ + N_BR + j + 2)
                ln_sqrt(2 * L)
                xt_evac(2 * L + 1, L, V_L1G, V_L1B)
                if L == 1:
                    break
                g0 = base + N_PROJ + N_BR + N_OUT
                for f in range(FT):
                    split(g0 + 2 * f + 2)
                    act.wait_ge(pe_chunk, g0 + 2 * f + 1)
                    if f >= 3:
                        act.wait_ge(ff_lo, f - 2)
                    nc.scalar.activation(fb[:, f % 3, :], bank[2 * (f % 2)][:, :], ACT.Tanh,
                                         scale=0.5).then_inc(ff_th, 1)
                    split(g0 + 2 * f + 3)
                    act.wait_ge(ff_h, f + 1)
                    nc.scalar.activation(hh[:, f, :], fb[:, f % 3, :], ACT.Copy).then_inc(ff_hi, 1)
                for k in range(N_DN):
                    split(g0 + N_GU + k + 2)
                ln_sqrt(1)
                xt_evac(2, L, V_L2G, V_L2B)
            act.wait_ge(rt_d, 1)
            nc.scalar.activation(etmp[:, 1, :], etmp[:, 0, :], ACT.Exp).then_inc(rt_e, 1)
            act.wait_ge(scattered, 16 * 2 * TT)

            def load_rows(j):
                act.dma_start(rows[:, :, :], xd[bass.ds(j * CAP, CAP)].rearrange("(s p) d -> p s d", p=P)
                              ).then_inc(rows_in, 16)

            def store_rows(j):
                act.dma_start(yd[bass.ds(j * CAP, CAP)].rearrange("(s p) d -> p s d", p=P), yrows[:, :, :]
                              ).then_inc(e_out, 16)

            def xg_evac(n):
                for q in range(2):
                    act.wait_ge(rows_tr, n * 2 + 2 * q + 1)
                    nc.scalar.activation(xg[:, 4 * q:4 * q + 2, :], bank[4 + 2 * q][:, :].rearrange(
                        "p (k n) -> p k n", k=2), ACT.Copy).then_inc(xg_a, 1)

            load_rows(0)
            xg_evac(0)
            act.wait_ge(rt_tab, 1)
            turns = act.value_load(tab[0:1, 24:25], min_val=NE, max_val=MAX_ITEMS)
            with act.Fori(0, turns) as j:
                act.wait_ge(rows_tr, 4 * j + 4)
                load_rows(j + 1)
                for f in range(FET):
                    act.wait_ge(e_used, j * ECH + 2 * (f + 1))
                    if f >= 3:
                        act.wait_ge(e_h, j * FET + (f - 2))
                    nc.scalar.activation(eb[:, f % 3, :], bank[f % 3][:, 0:CAP], ACT.Tanh, scale=0.5).then_inc(e_th, 1)
                for q in range(2):
                    act.wait_ge(rows_tr, 4 * j + (4 + 2 * q + 1))
                    nc.scalar.activation(xg[:, 4 * q:4 * q + 2, :], bank[4 + 2 * q][:, :].rearrange(
                        "p (k n) -> p k n", k=2), ACT.Copy).then_inc(xg_a, 1)
                for d in range(KD):
                    act.wait_ge(e_used, j * ECH + (2 * FET + d + 1))
                    nc.scalar.activation(yt[:, d, :], bank[d % 2][:, 0:CAP], ACT.Copy).then_inc(e_yt, 1)
                act.wait_ge(e_yr, j * KD + (KD + 1))
                store_rows(j)
            act.wait_ge(e_out, turns * 16 + 16)
            act.sem_inc(all_stored, 1)
            for tt in range(TT):
                act.wait_ge(ln_mv, 3 * TT + tt + 1)
                nc.scalar.activation(rstd[:, tt:tt + 1], mv[:, tt, 1:2], ACT.Sqrt,
                                     bias=eps[:, 0:1]).then_inc(ln_sd, 1)

        @block.vector
        def _(dve):
            step = Step(dve, dve_step)
            V = nc.vector

            def lo(g):
                if g >= N_DENSE:
                    return
                dve.wait_ge(hi_done, g + 1)
                V.tensor_tensor(wlo[:, g % SPL, :], raw[:, g % RAW, :], whi[:, g % SPL, :],
                                ALU.subtract).then_inc(lo_done, 1)

            def xt_low(n):
                for k in range(KD):
                    dve.wait_ge(xt_hi, n_xt[n] + k + 1)
                    V.tensor_tensor(xtl[:, k, :], xs[:, k % 2, :], xth[:, k, :], ALU.subtract).then_inc(xt_lo, 1)

            def layer_norm(n):
                for tt in range(TT):
                    V.bn_stats(stats[:, tt, 0, :], X[:, tt, 0:512])
                    step(V.bn_stats(stats[:, tt, 1, :], X[:, tt, 512:1024]))
                    V.bn_aggr(mv[:, tt, :], stats[:, tt, :, :]).then_inc(ln_mv, 1)
                for tt in range(TT):
                    dve.wait_ge(ln_sd, TT * n + tt + 1)
                    step(V.reciprocal(rstd[:, tt:tt + 1], rstd[:, tt:tt + 1]))
                    V.tensor_scalar(X[:, tt, :], X[:, tt, :], mv[:, tt, 0:1], rstd[:, tt:tt + 1],
                                    ALU.subtract, ALU.mult).then_inc(ln_norm, 1)

            def out_rows(base, per, n_first):
                for c in range(2):
                    for i in range(per):
                        lo(base + c * per + i + 2)
                    dve.wait_ge(pe_chunk, base + (c + 1) * per)
                    if n_first:
                        dve.wait_ge(x_affine, n_first)
                    for tt in range(TT):
                        cols = slice(c * 512, (c + 1) * 512)
                        ins = V.scalar_tensor_tensor(X[:, tt, cols], X[:, tt, cols], ALPHA,
                                                     bank[out_bank(c, tt, per)][:, :], ALU.mult, ALU.add)
                    ins.then_inc(z_done, 1)
                dve.wait_ge(z_done, z_base[0] + 2)
                z_base[0] += 2

            z_base = [0]

            def rope(L, i):
                dve.wait_ge(rms_sd, 5 * L + i + 1)
                g = vcol(L, V_KG if i == 4 else V_QG)
                r, x = rms[:, i % 2, :], qk[:, i, :]
                step(V.reciprocal(r, r))
                step(V.scalar_tensor_tensor(x, x, g, r, ALU.mult, ALU.mult))
                step(V.stream_shuffle(shuf[:, 0, :], x, [(q + 16) % 32 for q in range(32)]))
                V.tensor_tensor(halves(x), halves(x), cos2, ALU.mult)
                step(V.tensor_tensor(halves(shuf[:, 0, :]), halves(shuf[:, 0, :]), sin2, ALU.mult))
                V.tensor_tensor(x, x, shuf[:, 0, :], ALU.add).then_inc(roped, 1)

            def taps(L):
                for k in range(CK):
                    for ti in range(2):
                        src = hpad[:, ti, :, k:k + SEQ]
                        acc = halves(cv[:, ti, :])
                        w = vec[:, L, V_DW + ti * CK + k:V_DW + ti * CK + k + 1]
                        if k == 0:
                            step(V.tensor_scalar(acc, src, w, vcol(L, V_BDW + ti), ALU.mult, ALU.add))
                        else:
                            ins = V.scalar_tensor_tensor(acc, src, w, acc, ALU.mult, ALU.add)
                            if k == CK - 1:
                                ins.then_inc(conv_done, 1)
                            else:
                                step(ins)
                        yield

            def side(L, m, tap):
                if 2 <= m <= 6:
                    rope(L, m - 2)
                if m in (11, 12):
                    ti = m - 11
                    dve.wait_ge(proj_evac, N_PROJ * L + m)
                    x = hpad[:, ti, :, CPAD:CPAD + SEQ]
                    step(V.scalar_tensor_tensor(x, halves(glu[:, ti, :]), 1.0, x, ALU.add, ALU.mult))
                s = m - M_GATE
                if s >= 1 and s % 2 == 1 and s // 2 < 8:
                    u = s // 2
                    dve.wait_ge(sc_mm, 8 * L + u + 1)
                    for a in range(2):
                        ins = V.tensor_reduce(smx[:, 0, 2 * a:2 * a + 2],
                                              bank[3 + a][:, :].rearrange("p (q s) -> p q s", q=2), AX.X, ALU.max)
                    step(ins)
                    V.tensor_scalar(smx[:, 1, :], smx[:, 0, :], -HD ** -0.5, None, ALU.mult).then_inc(sc_max, 1)
                if s >= 1:
                    for _i in range(4):
                        next(tap, None)
                if s >= 1 and s % 2 == 1 and s // 2 < 8:
                    u = s // 2
                    dve.wait_ge(sc_exp, 8 * L + u + 1)
                    step(V.reciprocal(smx[:, 3, :], smx[:, 2, :]))
                    for q in range(4):
                        ins = V.tensor_scalar(prob[:, q, :], prob[:, q, :], smx[:, 3, q:q + 1], None, ALU.mult)
                    ins.then_inc(sc_norm, 1)
                if s == 2:
                    for ti in range(2):
                        dve.wait_ge(pool_hi, 2 * L + ti + 1)
                        V.tensor_tensor(pml[:, ti, :], pm32[:, ti, :], pmh[:, ti, :], ALU.subtract).then_inc(pool_lo, 1)
                if s >= 3 and s % 2 == 1 and s // 2 - 1 < 8:
                    u = s // 2 - 1
                    dve.wait_ge(p_tr, 8 * L + u + 1)
                    if u >= 1:
                        dve.wait_ge(pv_mm, 8 * L + u)
                    V.tensor_copy(probt[:, 1], bank[6][:, :].rearrange("p (s q) -> p s q", s=2)).then_inc(p_tb, 1)
                if s >= 4 and s % 2 == 0 and s // 2 - 2 < 8:
                    u = s // 2 - 2
                    b, mt = u // 4, u % 4
                    cols = slice(b * SEQ, (b + 1) * SEQ)
                    dve.wait_ge(att_hi, 8 * L + u + 1)
                    V.tensor_tensor(attl[:, mt, cols], att32[:, mt, cols], atth[:, mt, cols],
                                    ALU.subtract).then_inc(att_lo, 1)
                if s == 19:
                    dve.wait_ge(conv_mean, L + 1)
                    for ti in range(2):
                        V.tensor_tensor(cv[:, ti, :], cv[:, ti, :], bank[3][:, :], ALU.subtract).then_inc(conv_cent, 1)
                if s == 21:
                    dve.wait_ge(conv_sd, L + 1)
                    step(V.reciprocal(crs[:, 1, :], crs[:, 0, :]))
                    for ti in range(2):
                        V.tensor_tensor(cv[:, ti, :], cv[:, ti, :], crs[:, 1, :], ALU.mult).then_inc(conv_nrm, 1)
                if s == 22:
                    for ti in range(2):
                        dve.wait_ge(conv_z, 2 * L + ti + 1)
                        V.scalar_tensor_tensor(cv[:, ti, :], csq[:, ti, :], 1.0, cv[:, ti, :], ALU.add,
                                               ALU.mult).then_inc(conv_act, 1)

            V.memset(eps[:, 0:1], LN_EPS)
            V.memset(eps[:, 1:2], RMS_EPS)
            dve.wait_ge(in_small, 80)
            for L in range(DEPTH):
                V.tensor_scalar(hvec[:, L, 0:26], vec[:, L, V_BG:V_BG + 26], 0.5, None, ALU.mult)
                step(V.tensor_scalar(hvec[:, L, 26:30], vec[:, L, V_CG:V_CG + 4], 0.25, None, ALU.mult))
            V.tensor_scalar(hvec[:, :, 30:32], hvec[:, :, 0:2], 1.0, None, ALU.mult).then_inc(setup_done, 1)
            xt_low(0)
            lo(0)
            lo(1)
            for L in range(DEPTH):
                base = LAYER_BASE[L]
                tap = taps(L)
                for m in range(N_PROJ):
                    lo(base + m + 2)
                    side(L, m, tap)
                for ti in range(2):
                    dve.wait_ge(conv_hi, 2 * L + ti + 1)
                    V.tensor_tensor(cvl[:, ti, :], cv[:, ti, :], cvh[:, ti, :], ALU.subtract).then_inc(conv_lo, 1)
                for j in range(N_BR):
                    lo(base + N_PROJ + j + 2)
                    dve.wait_ge(pe_chunk, base + N_PROJ + j + 1)
                    dve.wait_ge(proj_evac, N_PROJ * (L + 1))
                    if j >= 2:
                        dve.wait_ge(mg_lo, KD * L + j - 1)
                    for i in range(3):
                        ins = V.scalar_tensor_tensor(mrg[:, j % 2, i, :], gates[:, 8 * i + j, :], 1.0,
                                                     bank[3 * (j % 2) + i][:, :], ALU.add, ALU.mult)
                    ins.then_inc(br_gated, 1)
                    dve.wait_ge(mg_hi, KD * L + j + 1)
                    V.tensor_tensor(xtl[:, j, :], mrg[:, j % 2, 0, :], xth[:, j, :], ALU.subtract).then_inc(mg_lo, 1)
                out_rows(base + N_PROJ + N_BR, N_OUT // 2, 2 * TT * L)
                layer_norm(2 * L)
                if L == 1:
                    break
                xt_low(1)
                g0 = base + N_PROJ + N_BR + N_OUT
                for f in range(FT):
                    lo(g0 + 2 * f + 2)
                    dve.wait_ge(ff_th, f + 1)
                    b = fb[:, f % 3, :]
                    step(V.scalar_tensor_tensor(b, b, 1.0, bank[2 * (f % 2)][:, :], ALU.add, ALU.mult))
                    lo(g0 + 2 * f + 3)
                    dve.wait_ge(pe_chunk, g0 + 2 * f + 2)
                    V.scalar_tensor_tensor(b, b, 0.5, bank[2 * (f % 2) + 1][:, :], ALU.mult, ALU.mult).then_inc(ff_h, 1)
                    dve.wait_ge(ff_hi, f + 1)
                    V.tensor_tensor(hl[:, f, :], b, hh[:, f, :], ALU.subtract).then_inc(ff_lo, 1)
                out_rows(g0 + N_GU, N_DN // 2, TT)
                layer_norm(1)
                xt_low(2)

            dve.wait_ge(rt_logit, 1)
            b0 = bank[0]
            step(V.tensor_tensor(lg[:, :, :], brt[:, :].unsqueeze(1).broadcast_to([P, TT, NE]),
                                 b0[:, 0:TT * NE].rearrange("p (t e) -> p t e", t=TT), ALU.add))
            for tt in range(TT):
                step(V.max(mx8[:, tt, :], lg[:, tt, :]))
                step(V.max_index(ix8[:, tt, :], mx8[:, tt, :], lg[:, tt, :]))
            step(V.tensor_copy(ixf[:, :, :], ix8[:, :, :]))
            i8 = cst[:, C_I8:C_I8 + 8]
            for k in range(2):
                step(V.tensor_tensor(pick[:, k], i8.unsqueeze(1).broadcast_to([P, TT, NE]),
                                     ixf[:, :, k:k + 1].broadcast_to([P, TT, NE]), ALU.is_equal))
            V.tensor_tensor(both[:, :, :], pick[:, 0], pick[:, 1], ALU.add).then_inc(rt_both, 1)
            V.tensor_tensor(etmp[:, 0, :], mx8[:, :, 1], mx8[:, :, 0], ALU.subtract).then_inc(rt_d, 1)
            dve.wait_ge(rt_e, 1)
            step(V.tensor_scalar(etmp[:, 2, :], etmp[:, 1, :], 1.0, None, ALU.add))
            step(V.reciprocal(mixk[:, 0, :], etmp[:, 2, :]))
            V.tensor_tensor(mixk[:, 1, :], etmp[:, 1, :], mixk[:, 0, :], ALU.mult).then_inc(rt_mix, 1)
            dve.wait_ge(rt_cnt, 1)
            b1 = bank[1]
            V.tensor_copy(pos[:, :, :], b1[:, 0:TT * NE].rearrange("p (t e) -> p t e", t=TT))
            step(V.tensor_copy(cnt[:, :], b1[:, TT * NE:TT * NE + NE]))
            over, cum, before, delta, n0, n1, one = (small[:, i, :] for i in range(7))
            V.memset(one, 1.0)
            V.tensor_scalar(n0, cnt[:, :], float(CAP), None, ALU.min)
            V.tensor_scalar(n1, cnt[:, :], float(-CAP), None, ALU.add)
            step(V.tensor_scalar(over, cnt[:, :], float(CAP), None, ALU.is_gt))
            step(V.tensor_tensor_scan(cum, one, over, 0.0, ALU.mult, ALU.add))
            step(V.tensor_tensor(before, cum, over, ALU.subtract))
            step(V.tensor_scalar(delta, before, float(CAP), float((NE - 1) * CAP), ALU.mult, ALU.add))
            e256 = cst[:, C_E256:C_E256 + 8]
            step(V.tensor_tensor(delta, delta, e256, ALU.subtract))
            step(V.tensor_scalar(row[:, :, :], pos[:, :, :], float(CAP), None, ALU.is_ge))
            step(V.tensor_tensor(row[:, :, :], row[:, :, :], delta.unsqueeze(1).broadcast_to([P, TT, NE]), ALU.mult))
            step(V.tensor_tensor(row[:, :, :], row[:, :, :], pos[:, :, :], ALU.add))
            step(V.tensor_tensor(row[:, :, :], row[:, :, :], e256.unsqueeze(1).broadcast_to([P, TT, NE]), ALU.add))
            for k in range(2):
                step(V.tensor_tensor(rtmp[:, :, :], row[:, :, :], pick[:, k], ALU.mult))
                step(V.tensor_reduce(rowk[:, k, :], rtmp[:, :, :], AX.X, ALU.add))
            step(V.tensor_copy(ridx[:, :, :], rowk[:, :, :]))
            step(V.memset(tabf[:, :], 0.0))
            V.tensor_copy(tabf[:, 0:8], i8)
            V.tensor_copy(tabf[:, 12:20], n0)
            V.tensor_scalar(tabf[:, 24:25], cum[:, 7:8], float(NE), None, ALU.add)
            step(V.tensor_tensor(t48[:, :, :], before.unsqueeze(1).broadcast_to([P, 4, NE]),
                                 cst[:, C_I4:C_I4 + 4].unsqueeze(2).broadcast_to([P, 4, NE]), ALU.is_equal))
            step(V.tensor_tensor(t48[:, :, :], t48[:, :, :], over.unsqueeze(1).broadcast_to([P, 4, NE]), ALU.mult))
            for what, dst in ((i8, 8), (n1, 20)):
                step(V.tensor_tensor(rtmp[:, :, :], t48[:, :, :], what.unsqueeze(1).broadcast_to([P, 4, NE]), ALU.mult))
                step(V.tensor_reduce(tabf[:, dst:dst + 4], rtmp[:, :, :], AX.X, ALU.add))
            items = tabf[:, 12:24]
            for i, n in enumerate(WIDTHS[:-1]):
                if i == 0:
                    step(V.tensor_scalar(wcls[:, 0, :], items, float(n), None, ALU.is_gt))
                else:
                    step(V.tensor_scalar(wcls[:, 1, :], items, float(n), None, ALU.is_gt))
                    step(V.tensor_tensor(wcls[:, 0, :], wcls[:, 0, :], wcls[:, 1, :], ALU.add))
            step(V.tensor_copy(items, wcls[:, 0, :]))
            V.tensor_copy(tab[:, :], tabf[:, :]).then_inc(rt_tab, 1)

            def xg_evac():
                for q in range(2):
                    dve.wait_ge(rows_tr, 2 * q + 2)
                    V.tensor_copy(xg[:, 4 * q + 2:4 * q + 4, :], bank[5 + 2 * q][:, :].rearrange(
                        "p (k n) -> p k n", k=2)).then_inc(xg_b, 1)

            dve.wait_ge(rt_tab, 1)
            turns = dve.value_load(tab[0:1, 24:25], min_val=NE, max_val=MAX_ITEMS)
            xg_evac()
            dve.sem_inc(e_yr, 1)
            t_base = step.n
            with dve.Fori(0, turns) as j:
                step.turn(j * FET + t_base)
                for f in range(FET):
                    dve.wait_ge(e_th, j * FET + (f + 1))
                    b = eb[:, f % 3, :]
                    step(V.scalar_tensor_tensor(b, b, 1.0, bank[f % 3][:, 0:CAP], ALU.add, ALU.mult))
                    V.scalar_tensor_tensor(eh[:, f, :], b, 0.5, bank[f % 3][:, CAP:2 * CAP], ALU.mult,
                                           ALU.mult).then_inc(e_h, 1)
                for q in range(2):
                    dve.wait_ge(rows_tr, 4 * j + (4 + 2 * q + 2))
                    V.tensor_copy(xg[:, 4 * q + 2:4 * q + 4, :], bank[5 + 2 * q][:, :].rearrange(
                        "p (k n) -> p k n", k=2)).then_inc(xg_b, 1)
                for d in range(KD):
                    dve.wait_ge(e_ytr, j * KD + (d + 1))
                    if d == 0:
                        dve.wait_ge(e_out, 16 * j + 16)
                    V.tensor_copy(yrows[:, :, d * P:(d + 1) * P], bank[2 + d % 2][:, 0:2 * P].rearrange(
                        "p (s n) -> p s n", s=2)).then_inc(e_yr, 1)
            final = sem("final_step")
            fin = Step(dve, final)
            dve.wait_ge(rt_mix, 1)
            for tt in range(TT):
                dve.wait_ge(gathered, 16 * 2 * TT)
                fin(V.tensor_scalar(yg[:, 0, tt, :], yg[:, 0, tt, :], mixk[:, 0, tt:tt + 1], None, ALU.mult))
                fin(V.scalar_tensor_tensor(yg[:, 0, tt, :], yg[:, 1, tt, :], mixk[:, 1, tt:tt + 1], yg[:, 0, tt, :],
                                           ALU.mult, ALU.add))
                fin(V.scalar_tensor_tensor(X[:, tt, :], X[:, tt, :], ALPHA, yg[:, 0, tt, :], ALU.mult, ALU.add))
                V.bn_stats(stats[:, tt, 0, :], X[:, tt, 0:512])
                fin(V.bn_stats(stats[:, tt, 1, :], X[:, tt, 512:1024]))
                V.bn_aggr(mv[:, tt, :], stats[:, tt, :, :]).then_inc(ln_mv, 1)
            dve.wait_ge(in_ln, 64)
            for tt in range(TT):
                dve.wait_ge(ln_sd, 3 * TT + tt + 1)
                fin(V.reciprocal(rstd[:, tt:tt + 1], rstd[:, tt:tt + 1]))
                fin(V.tensor_scalar(X[:, tt, :], X[:, tt, :], mv[:, tt, 0:1], rstd[:, tt:tt + 1], ALU.subtract,
                                    ALU.mult))
                fin(V.tensor_tensor(X[:, tt, :], X[:, tt, :], lngb[:, 0, :], ALU.mult))
                V.tensor_tensor(X[:, tt, :], X[:, tt, :], lngb[:, 1, :], ALU.add).then_inc(y_ready, 1)

        @block.gpsimd
        def _(pool):
            G = nc.gpsimd
            step = Step(pool, pool_step)
            G.memset(zero[:, :], 0.0).then_inc(zero_set, 1)
            pool.wait_ge(zero_set, 1)
            for i in range(N_ROWS // 256):
                pool.dma_start(xd[i * 256:(i + 1) * 256].rearrange("(p s) d -> p (s d)", p=P),
                               zero[:, :]).then_inc(zeroed, 16)
            for i in range(NE + 1, N_ROWS // 256):
                pool.dma_start(yd[i * 256:(i + 1) * 256].rearrange("(p s) d -> p (s d)", p=P),
                               zero[:, :]).then_inc(zeroed, 16)
            pool.wait_ge(zeroed, 16 * (N_ROWS // 128 - NE - 1))

            def affine(n):
                pool.wait_ge(in_ln, 16 * (n + 1))
                for tt in range(TT):
                    pool.wait_ge(xt_tr, n_xt[n + 1] + KD)
                    step(G.tensor_tensor(X[:, tt, :], X[:, tt, :], lngb[:, 0, :], ALU.mult))
                    G.tensor_tensor(X[:, tt, :], X[:, tt, :], lngb[:, 1, :], ALU.add).then_inc(x_affine, 1)

            for L in range(DEPTH):
                pool.wait_ge(xt_lo, n_xt[2 * L] + KD)
                for lo_, hi_ in ((0, PPAD), (PPAD + SEQ, PW)):
                    G.memset(upad[:, :, :, lo_:hi_], 0.0)
                G.memset(hpad[:, :, :, 0:CPAD], 0.0)
                G.memset(hpad[:, :, :, CPAD + SEQ:CW], 0.0).then_inc(pads, 1)
                if L == 1:
                    affine(1)
                pool.wait_ge(proj_evac, N_PROJ * L + M_CA)
                for ti in range(2):
                    G.tensor_tensor(psa[:, ti, :, 1:PW], upad[:, ti, :, 0:PW - 1], upad[:, ti, :, 1:PW],
                                    ALU.add).then_inc(pool_step, 1)
                step.n += 2
                pool.wait_ge(pool_step, step.n)
                for ti in range(2):
                    G.tensor_tensor(psb[:, ti, :, 2:PW - 1], psa[:, ti, :, 1:PW - 2], psa[:, ti, :, 3:PW],
                                    ALU.add).then_inc(pool_step, 1)
                step.n += 2
                pool.wait_ge(pool_step, step.n)
                step(G.tensor_tensor(psa[:, 1, :, 4:PW - 3], psb[:, 1, :, 2:PW - 5], psb[:, 1, :, 6:PW - 1], ALU.add))
                step(G.tensor_tensor(psb[64:P, 1, :, 8:PW - 8], psa[64:P, 1, :, 4:PW - 12], psa[64:P, 1, :, 12:PW - 4],
                                     ALU.add))
                for ti in range(2):
                    for h in range(2):
                        ps = slice(64 * h, 64 * h + 64)
                        inv = cst[ps, C_INV + ti * SEQ:C_INV + (ti + 1) * SEQ].unsqueeze(1).broadcast_to([64, NB, SEQ])
                        o_ = halves(pooled[ps, ti, :])
                        src = (psa, psb)[h]
                        step(G.tensor_tensor(o_, src[ps, ti, :, PPAD:PPAD + SEQ], inv, ALU.mult))
                        ins = G.tensor_tensor(o_, o_, upad[ps, ti, :, PPAD:PPAD + SEQ], ALU.subtract)
                        if ti == 1 and h == 1:
                            ins.then_inc(pool_in, 1)
                        else:
                            step(ins)
                for j in range(N_BR):
                    pool.wait_ge(br_gated, KD * L + j + 1)
                    m = mrg[:, j % 2]
                    step(G.tensor_tensor(m[:, 0, :], m[:, 0, :], m[:, 1, :], ALU.add))
                    G.tensor_tensor(m[:, 0, :], m[:, 0, :], m[:, 2, :], ALU.add).then_inc(br_sum, 1)
                affine(2 * L)
            pool.wait_ge(rt_tab, 1)
            pool.wait_ge(x_affine, 3 * TT)
            for tt in range(TT):
                for k in range(2):
                    pool.indirect_dma_start(out=xd, out_offset=bass.IndirectOffsetOnAxis(
                        ap=ridx[:, k, tt:tt + 1], axis=0), in_=X[:, tt, :], in_offset=None).then_inc(scattered, 16)
            pool.wait_ge(all_stored, 1)
            for tt in range(TT):
                for k in range(2):
                    pool.indirect_dma_start(out=yg[:, k, tt, :], out_offset=None, in_=yd,
                                            in_offset=bass.IndirectOffsetOnAxis(ap=ridx[:, k, tt:tt + 1], axis=0)
                                            ).then_inc(gathered, 16)

        @block.tensor
        def _(pe):
            mm = nc.tensor.matmul

            def transposes(n):
                if n == 0:
                    pe.wait_ge(in_x, 32)
                    pe.wait_ge(in_small, 80)
                else:
                    pe.wait_ge(ln_norm, TT * n)
                for k in range(KD):
                    for tt in range(TT):
                        last = nc.tensor.transpose(bank[k][:, tt * P:(tt + 1) * P], X[:, tt, k * P:(k + 1) * P], ident)
                    last.then_inc(xt_tr, 1)

            def three(out, wh, wl, xh, xl, first, last):
                mm(out, wh, xh, start=first, stop=False)
                mm(out, wh, xl, start=False, stop=False)
                return mm(out, wl, xh, start=False, stop=last)

            def wtile(g, k):
                return whi[:, g % SPL, k * P:(k + 1) * P], wlo[:, g % SPL, k * P:(k + 1) * P]

            def features(g, out):
                pe.wait_ge(lo_done, g + 1)
                for k in range(KD):
                    wh, wl = wtile(g, k)
                    ins = three(out, wh, wl, xth[:, k, :], xtl[:, k, :], k == 0, k == KD - 1)
                ins.then_inc(pe_chunk, 1)

            def token_rows(base, per, ah, al, ready):
                for c in range(2):
                    for i in range(per):
                        g = base + c * per + i
                        pe.wait_ge(lo_done, g + 1)
                        for kk in range(2):
                            k = 2 * i + kk
                            if c == 0:
                                ready(k)
                            wh = whi[:, g % SPL, kk * 512:(kk + 1) * 512]
                            wl = wlo[:, g % SPL, kk * 512:(kk + 1) * 512]
                            for tt in range(TT):
                                out = bank[out_bank(c, tt, per)][:, :]
                                t = slice(tt * P, (tt + 1) * P)
                                mm(out, ah[:, k, t], wh, start=(k == 0), stop=False)
                                mm(out, ah[:, k, t], wl, start=False, stop=False)
                                ins = mm(out, al[:, k, t], wh, start=False, stop=(k == 2 * per - 1))
                        ins.then_inc(pe_chunk, 1)

            def side(L, m):
                if 1 <= m <= 5:
                    i = m - 1
                    pe.wait_ge(proj_evac, N_PROJ * L + i + 1)
                    if i >= 2:
                        pe.wait_ge(rms_sd, 5 * L + i - 1)
                    mm(bank[3 + i % 2][:, :], cst[:, C_BLK:C_BLK + P], sq[:, i % 2, :], start=True,
                       stop=True).then_inc(rms_ms, 1)
                if m == 6:
                    pe.wait_ge(proj_evac, N_PROJ * L + M_V + 1)
                    for tt in range(TT):
                        ins = nc.tensor.transpose(bank[5][:, tt * P:(tt + 1) * P], vt[:, tt * P:(tt + 1) * P], ident)
                    ins.then_inc(v_tr, 1)
                s = m - M_GATE
                if s == 1:
                    pe.wait_ge(pool_in, L + 1)
                    pe.wait_ge(v_tok, L + 1)
                    for ti in range(2):
                        mm(bank[5 + ti][:, :], mixw[:, L, ti, :], pooled[:, ti, :], start=True,
                           stop=True).then_inc(pool_mm, 1)
                if s >= 2 and s % 2 == 0 and s // 2 - 1 < 8:
                    u = s // 2 - 1
                    pe.wait_ge(sc_norm, 8 * L + u + 1)
                    if u == 0:
                        pe.wait_ge(pool_hi, 2 * L + 2)
                    else:
                        pe.wait_ge(p_ta, 8 * L + u)
                        pe.wait_ge(p_tb, 8 * L + u)
                    for a in range(2):
                        for st in range(2):
                            for qt in range(2):
                                o_ = st * SEQ + qt * P
                                ins = nc.tensor.transpose(bank[5 + a][:, o_:o_ + P],
                                                          prob[:, 2 * a + qt, st * P:(st + 1) * P], ident)
                    ins.then_inc(p_tr, 1)
                if s >= 0 and s % 2 == 0 and s // 2 < 8:
                    u = s // 2
                    b, mt = u // 4, u % 4
                    pe.wait_ge(roped, 5 * L + 5)
                    if u == 0:
                        pe.wait_ge(rms_sd, 5 * L + 5)
                    if u >= 1:
                        pe.wait_ge(sc_exp, 8 * L + u)
                    for a in range(2):
                        h = slice(64 * a, 64 * a + 64)
                        for qt in range(2):
                            q0 = b * SEQ + qt * P
                            ins = mm(bank[3 + a][:, qt * SEQ:(qt + 1) * SEQ], qk[h, mt, q0:q0 + P],
                                     qk[h, 4, b * SEQ:(b + 1) * SEQ], start=True, stop=True)
                    ins.then_inc(sc_mm, 1)
                if s >= 3 and s % 2 == 1 and s // 2 - 1 < 8:
                    u = s // 2 - 1
                    b = u // 4
                    pe.wait_ge(p_ta, 8 * L + u + 1)
                    pe.wait_ge(p_tb, 8 * L + u + 1)
                    if u >= 1:
                        pe.wait_ge(att_full, 8 * L + u)
                    for a in range(2):
                        h = slice(64 * a, 64 * a + 64)
                        for st in range(2):
                            ins = mm(bank[7][h, 0:SEQ], vtok[:, 2 * b + st, h], probt[:, a, st, :],
                                     start=(st == 0), stop=(st == 1))
                    ins.then_inc(pv_mm, 1)
                if s == 18:
                    pe.wait_ge(conv_done, 2 * L + 2)
                    for ti in range(2):
                        ins = mm(bank[3][:, :], cst[:, C_MEAN:C_MEAN + P], cv[:, ti, :], start=(ti == 0),
                                 stop=(ti == 1))
                    ins.then_inc(conv_mean, 1)
                if s == 20:
                    pe.wait_ge(conv_sq, L + 1)
                    for ti in range(2):
                        ins = mm(bank[4][:, :], cst[:, C_MEAN:C_MEAN + P], csq[:, ti, :], start=(ti == 0),
                                 stop=(ti == 1))
                    ins.then_inc(conv_var, 1)

            transposes(0)
            for L in range(DEPTH):
                base = LAYER_BASE[L]
                pe.wait_ge(xt_lo, n_xt[2 * L] + KD)
                for m in range(N_PROJ):
                    if m >= 3:
                        pe.wait_ge(proj_evac, N_PROJ * L + m - 2)
                    features(base + m, bank[m % 3][:, :])
                    side(L, m)
                pe.wait_ge(att_lo, 8 * (L + 1))
                pe.wait_ge(pool_lo, 2 * (L + 1))
                pe.wait_ge(proj_evac, N_PROJ * (L + 1))
                pe.wait_ge(conv_lo, 2 * (L + 1))
                for j in range(N_BR):
                    g = base + N_PROJ + j
                    pe.wait_ge(lo_done, g + 1)
                    if j >= 2:
                        pe.wait_ge(br_gated, KD * L + j - 1)
                    k = 0
                    for i, (ah, al, n) in enumerate(((atth, attl, 4), (pmh, pml, 2), (cvh, cvl, 2))):
                        for t in range(n):
                            wh, wl = wtile(g, k)
                            ins = three(bank[3 * (j % 2) + i][:, :], wh, wl, ah[:, t, :], al[:, t, :], t == 0,
                                        t == n - 1)
                            k += 1
                    ins.then_inc(pe_chunk, 1)
                pe.wait_ge(br_gated, KD * L + KD)

                def merged(k, L=L):
                    pe.wait_ge(mg_lo, KD * L + k + 1)

                token_rows(base + N_PROJ + N_BR, N_OUT // 2, xth, xtl, merged)
                if L == 1:
                    break
                transposes(1)
                pe.wait_ge(xt_lo, n_xt[1] + KD)
                g0 = base + N_PROJ + N_BR + N_OUT
                for f in range(FT):
                    if f >= 2:
                        pe.wait_ge(ff_h, f - 1)
                    features(g0 + 2 * f, bank[2 * (f % 2)][:, :])
                    features(g0 + 2 * f + 1, bank[2 * (f % 2) + 1][:, :])

                def hidden(k):
                    pe.wait_ge(ff_lo, k + 1)

                token_rows(g0 + N_GU, N_DN // 2, hh, hl, hidden)
                transposes(2)

            pe.wait_ge(ln_norm, 3 * TT)
            for k in range(KD):
                for tt in range(TT):
                    last = nc.tensor.transpose(bank[k][:, tt * P:(tt + 1) * P], X[:, tt, k * P:(k + 1) * P], ident)
                last.then_inc(xt_tr, 1)
            pe.wait_ge(xt_full, KD)
            for tt in range(TT):
                for k in range(KD):
                    ins = mm(bank[0][:, tt * NE:(tt + 1) * NE], xt32[:, k, tt * P:(tt + 1) * P], wrt[:, k, :],
                             start=(k == 0), stop=(k == KD - 1))
            ins.then_inc(rt_logit, 1)
            pe.wait_ge(rt_both, 1)
            for tt in range(TT):
                for i in range(tt):
                    mm(bank[1][:, tt * NE:(tt + 1) * NE], cst[:, C_ONE:C_ONE + P], both[:, i, :], start=(i == 0),
                       stop=False)
                mm(bank[1][:, tt * NE:(tt + 1) * NE], cst[:, C_TRI:C_TRI + P], both[:, tt, :], start=(tt == 0),
                   stop=True)
            for i in range(TT):
                ins = mm(bank[1][:, TT * NE:TT * NE + NE], cst[:, C_ONE:C_ONE + P], both[:, i, :], start=(i == 0),
                         stop=(i == TT - 1))
            ins.then_inc(rt_cnt, 1)
            pe.wait_ge(rt_tab, 1)
            turns = pe.value_load(tab[0:1, 24:25], min_val=NE, max_val=MAX_ITEMS)

            def rows_to_features():
                for kp in range(4):
                    for kk in range(2):
                        for st in range(2):
                            o_ = kk * CAP + st * P
                            k = 2 * kp + kk
                            ins = nc.tensor.transpose(bank[4 + kp][:, o_:o_ + P], rows[:, st, k * P:(k + 1) * P], ident)
                    ins.then_inc(rows_tr, 1)

            pe.wait_ge(rows_in, 16)
            rows_to_features()
            with pe.Fori(0, turns) as j:
                pe.wait_ge(xg_a, 2 * j + 2)
                pe.wait_ge(xg_b, 2 * j + 2)
                lap = j * (16 * (ECH // ERING))
                width = pe.value_load(tab[0:1, bass.ds(j + 12, 1)], min_val=0, max_val=len(WIDTHS) - 1)

                def back(d):
                    pe.wait_ge(e_yt, j * KD + (d + 1))
                    if d >= 2:
                        pe.wait_ge(e_yr, j * KD + d)
                    for st in range(2):
                        ins = nc.tensor.transpose(bank[2 + d % 2][:, st * P:(st + 1) * P],
                                                  yt[:, d, st * P:(st + 1) * P], ident)
                    ins.then_inc(e_ytr, 1)

                def item(n):
                    for f in range(FET):
                        if f == 2:
                            pe.wait_ge(e_yr, j * KD + 1)
                        if f >= 3:
                            pe.wait_ge(e_h, j * FET + (f - 2))
                        for w in range(2):
                            k = 2 * f + w
                            pe.wait_ge(in_e[k % ERING], lap + 16 * (k // ERING + 1))
                            for t in range(KD):
                                ins = mm(bank[f % 3][:, w * CAP:w * CAP + n], ring[:, k % ERING, t * P:(t + 1) * P],
                                         xg[:, t, 0:n], start=(t == 0), stop=(t == KD - 1))
                            ins.then_inc(e_used, 1)
                    pe.wait_ge(rows_in, 16 * j + 32)
                    rows_to_features()
                    pe.wait_ge(e_h, j * FET + FET)
                    for d in range(KD):
                        k = 2 * FET + d
                        if d >= 2:
                            pe.wait_ge(e_yt, j * KD + (d - 1))
                        pe.wait_ge(in_e[k % ERING], lap + 16 * (k // ERING + 1))
                        for t in range(FET):
                            ins = mm(bank[d % 2][:, 0:n], ring[:, k % ERING, t * P:(t + 1) * P], eh[:, t, 0:n],
                                     start=(t == 0), stop=(t == FET - 1))
                        ins.then_inc(e_used, 1)
                        if d >= 1:
                            back(d - 1)
                    back(KD - 1)

                for c, n in enumerate(WIDTHS):
                    with pe.If(width == c):
                        item(n)


def tiles_by_column(w):
    k, n = w.shape
    return np.ascontiguousarray(w.reshape(k // P, P, n // P, P).transpose(2, 1, 0, 3)).reshape(n // P, P, k)


def rows_by_half(w):
    k = w.shape[0]
    return np.ascontiguousarray(w.reshape(k // 256, 2, P, 2, 512).transpose(3, 0, 2, 1, 4)).reshape(-1, P, CH)


def heads_paired(w, axis):
    order = [h for i in range(4) for h in (i, i + 4)]
    parts = np.split(w, 8, axis=axis)
    return np.concatenate([parts[h] for h in order], axis=axis)


def kernel(**inputs):
    import concourse.bacc as bacc
    from concourse.bass_utils import run_bass_kernel_spmd

    a = {k: np.asarray(v) for k, v in inputs.items()}

    def col(v):
        return np.ascontiguousarray(v.reshape(-1, P).T)

    stream = []
    for L in range(DEPTH):
        w = a["w_in"][L]
        w = np.concatenate([heads_paired(w[:, :512], 1), w[:, 512:]], axis=1)
        stream.append(tiles_by_column(w))
        wb = np.concatenate([heads_paired(a["w_attn_out"][L], 0), a["w_pool_out"][L], a["w_conv_out"][L]], axis=0)
        stream.append(tiles_by_column(wb))
        stream.append(rows_by_half(a["w_out"][L]))
        if L == 0:
            gu = np.stack([tiles_by_column(a["w_ff_gate"][0]), tiles_by_column(a["w_ff_up"][0])], axis=1)
            stream.append(gu.reshape(-1, P, CH))
            stream.append(rows_by_half(a["w_ff_down"][0]))
    dense = np.concatenate(stream, axis=0)
    gus, dns = [], []
    for e in range(NE):
        gu = np.stack([tiles_by_column(a["w_e_gate"][0, e]), tiles_by_column(a["w_e_up"][0, e])], axis=1)
        gus.append(gu.reshape(-1, P, CH))
        dns.append(tiles_by_column(a["w_e_down"][0, e]))
    vecs = np.zeros((P, DEPTH, V_END), np.float32)
    mix = np.zeros((P, DEPTH, 2, P), np.float32)
    for L in range(DEPTH):
        vecs[:, L, V_QG] = np.tile(a["q_norm_g"][L], 2)
        vecs[:, L, V_KG] = np.tile(a["k_norm_g"][L], 2)
        for name, c, n in (("b_gate", V_BG, 24), ("pool_scale", V_PS, 2), ("b_dw", V_BDW, 2), ("conv_ln_g", V_CG, 2),
                           ("conv_ln_b", V_CB, 2), ("ln1_g", V_L1G, 8), ("ln1_b", V_L1B, 8), ("ln2_g", V_L2G, 8),
                           ("ln2_b", V_L2B, 8)):
            vecs[:, L, c:c + n] = col(a[name][L])
        for ti in range(2):
            vecs[:, L, V_DW + ti * CK:V_DW + (ti + 1) * CK] = a["w_dw"][L][:, ti * P:(ti + 1) * P].T
            for h in range(2):
                s = slice(64 * h, 64 * h + 64)
                mix[s, L, ti, s] = a["w_pool_mix"][L, 2 * ti + h]
    lnrow = np.stack([np.stack([a[f"ln{i}_g"][L], a[f"ln{i}_b"][L]]) for L in range(DEPTH) for i in (1, 2)])
    ins = {
        "x0": a["x_prompt"], "x1": a["x_sample"], "dense_w": dense, "expert_gu": np.concatenate(gus),
        "expert_dn": np.concatenate(dns), "consts": shape_constants(), "vecs": vecs, "mix": mix, "lnrow": lnrow,
        "wr": a["w_router"], "br": a["b_router"],
    }
    ins = {k: np.ascontiguousarray(v) for k, v in ins.items()}
    nc = bacc.Bacc("TRN2", target_bir_lowering=False, num_devices=1)
    aps = {k: nc.dram_tensor(k, v.shape, mybir.dt.from_np(v.dtype), kind="ExternalInput").ap()
           for k, v in ins.items()}
    xd = nc.dram_tensor("item_rows", (N_ROWS, D), F32, kind="Internal").ap()
    yd = nc.dram_tensor("item_results", (N_ROWS, D), F32, kind="Internal").ap()
    y0 = nc.dram_tensor("y0", (1, SEQ, D), F32, kind="ExternalOutput").ap()
    y1 = nc.dram_tensor("y1", (1, SEQ, D), F32, kind="ExternalOutput").ap()
    build_trunk(nc, xd=xd, yd=yd, y0=y0, y1=y1, **aps)
    r = run_bass_kernel_spmd(nc, [ins], core_ids=[0])
    return r.results[0]["y0"], r.results[0]["y1"]
```

```python
from contextlib import ExitStack

import numpy as np

import concourse.bass as bass
from concourse import mybir

F32 = mybir.dt.float32
F32R = mybir.dt.float32r
BF16 = mybir.dt.bfloat16
U32 = mybir.dt.uint32
I32 = mybir.dt.int32
ALU = mybir.AluOpType
ACT = mybir.ActivationFunctionType
AX = mybir.AxisListType

P = 128
DEPTH = 2
NB, SEQ = 2, 256
TOK = NB * SEQ
TT = TOK // P
D = 1024
KD = D // P
HD = 64
POOL_WINDOWS = (2, 4, 8, 16)
CK = 31
CPAD = CK // 2
PPAD = 8
FF = 2816
FT = FF // P
NE = 8
FE = 1408
FET = FE // P
ALPHA = (2 * DEPTH) ** 0.25
LN_EPS = 1e-5
RMS_EPS = 1e-6
GRID_W = 64

CH = 1024
N_PROJ, N_BR, N_OUT, N_GU, N_DN = 36, 8, 8, 2 * FT, FT
M_V, M_POOL, M_CA, M_CB, M_GATE = 5, 6, 8, 10, 12
LAYER_BASE = (0, N_PROJ + N_BR + N_OUT + N_GU + N_DN)
N_DENSE = LAYER_BASE[1] + N_PROJ + N_BR + N_OUT
RAW, SPL = 4, 3
ROPE_AT = (2, 3, 5, 7, 9)

CAP = 256
MAX_ITEMS = 11
N_ROWS = (MAX_ITEMS + 1) * CAP
ECH = 2 * FET + KD
DCH = FET * P
ERING = 15
WIDTHS = (128, 144, 160, 176, 192, 224, CAP)

C_ID, C_BLK, C_MEAN, C_ONE, C_TRI = 0, 128, 256, 384, 512
C_COS, C_SIN, C_INV = 640, 896, 1152
C_I8, C_E256, C_I4 = 1664, 1672, 1680
C_END = 1684

V_QG, V_KG, V_BG, V_PS, V_BDW, V_CG, V_CB, V_DW = 0, 1, 2, 26, 28, 30, 32, 34
V_L1G, V_L1B, V_L2G, V_L2B = 96, 104, 112, 120
V_END = 128


def shape_constants():
    c = np.zeros((P, C_END), np.float32)
    c[:, C_ID:C_ID + P] = np.eye(P)
    for h in range(2):
        c[64 * h:64 * h + 64, C_BLK + 64 * h:C_BLK + 64 * h + 64] = 1.0 / HD
    c[:, C_MEAN:C_MEAN + P] = 1.0 / 256
    c[:, C_ONE:C_ONE + P] = 1.0
    c[:, C_TRI:C_TRI + P] = np.triu(np.ones((P, P)), 1)
    nf = HD // 4
    inv = np.float32(10000.0) ** (-np.arange(nf, dtype=np.float32) / np.float32(nf))
    t = np.arange(SEQ)
    for p in range(P):
        half = (p % HD) // 32
        ang = (t // GRID_W if half == 0 else t % GRID_W).astype(np.float32) * inv[p % 16]
        c[p, C_COS:C_COS + SEQ] = np.cos(ang)
        c[p, C_SIN:C_SIN + SEQ] = np.sin(ang) * (-1.0 if p % 32 < 16 else 1.0)
        for ti in range(2):
            w = POOL_WINDOWS[2 * ti + p // 64]
            n = np.clip(t + w - w // 2, 0, SEQ) - np.clip(t - w // 2, 0, SEQ)
            c[p, C_INV + ti * SEQ:C_INV + (ti + 1) * SEQ] = 1.0 / n
    c[:, C_I8:C_I8 + 8] = np.arange(8)
    c[:, C_E256:C_E256 + 8] = np.arange(8) * CAP
    c[:, C_I4:C_I4 + 4] = np.arange(4)
    return c


class Step:

    def __init__(self, eng, sem):
        self.eng, self.sem, self.n, self.base = eng, sem, 0, 0

    def turn(self, base):
        self.base, self.n = base, 0

    def __call__(self, ins):
        self.n += 1
        ins.then_inc(self.sem, 1)
        self.eng.wait_ge(self.sem, self.base + self.n)


def build_trunk(nc, x0, x1, dense_w, expert_gu, expert_dn, consts, slots, vecs, mix, lnrow, wr, br, xd, yd, y0, y1):
    ctx = ExitStack()
    with ctx:
        def sem(name):
            return ctx.enter_context(nc.semaphore(name))

        top = [16512]

        def at(name, shape, dt, offset=None):
            size = 4 * int(np.prod(shape[1:]))
            size = (size + 31) // 32 * 32
            if offset is None:
                offset = top[0]
                top[0] += size
            return nc.alloc_sbuf_tensor_at(name, shape, dt, offset=offset)

        def here():
            return top[0]

        cst = at("cst", [P, C_END], F32)
        vec = at("vec", [P, DEPTH, V_END], F32)
        hvec = at("hvec", [P, DEPTH, 32], F32)
        mixw = at("mixw", [P, DEPTH, 2, P], F32)
        eps = at("eps", [P, 2], F32)
        wrt = at("wrt", [P, KD, NE], F32)
        brt = at("brt", [P, NE], F32)
        stats = at("stats", [P, TT, 2, 6], F32)
        mv = at("mv", [P, TT, 2], F32)
        rstd = at("rstd", [P, TT], F32)
        nmr = at("nmr", [P, TT], F32)
        smx = at("smx", [P, 4, 4], F32)
        lngb = at("lngb", [P, 2, D], F32)
        X = at("X", [P, TT, D], F32)
        o_xth = here()
        xth = at("xth", [P, KD, TOK], F32R)
        xt32 = at("xt32", [P, KD, TOK], F32, o_xth)
        xtl = at("xtl", [P, KD, TOK], F32R)
        raw = at("raw", [P, RAW, CH], F32)
        whi = at("whi", [P, SPL, CH], F32R)
        wlo = at("wlo", [P, SPL, CH], F32R)
        o_m = here()
        gates = at("gates", [P, 24, TOK], F32)
        o = o_m + 10 * 2048
        rms = at("rms", [P, 2, TOK], F32, o)
        shuf = at("shuf", [P, 1, TOK], F32, o + 4096)
        sq = at("sq", [P, 2, TOK], F32, o + 6144)
        o = o_m + 15 * 2048
        PW = SEQ + 2 * PPAD
        upad = at("upad", [P, 2, NB, PW], F32, o)
        psa = at("psa", [P, 2, NB, PW], F32, o + 16 * PW)
        psb = at("psb", [P, 2, NB, PW], F32, o + 32 * PW)
        pooled = at("pooled", [P, 2, TOK], F32, o + 48 * PW)
        assert o + 48 * PW + 4096 <= here()
        o_q = here()
        qk = at("qk", [P, 5, TOK], F32)
        atth = at("atth", [P, 4, TOK], F32R, o_q)
        o_s = here()
        prob = at("prob", [P, 4, SEQ], F32)
        probt = at("probt", [P, 2, 2, SEQ], F32)
        vt = at("vt", [P, TOK], F32)
        vtok = at("vtok", [P, TT, P], F32)
        glu = at("glu", [P, 2, TOK], F32, o_s)
        csq = at("csq", [P, 2, TOK], F32, o_s)
        crs = at("crs", [P, 2, TOK], F32, o_s + 4096)
        mrg = at("mrg", [P, 2, 3, TOK], F32, o_s)
        o_al = here()
        att32 = at("att32", [P, 4, TOK], F32)
        attl = at("attl", [P, 4, TOK], F32R, o_al)
        o_pl = here()
        pm32 = at("pm32", [P, 2, TOK], F32)
        pml = at("pml", [P, 2, TOK], F32R, o_pl)
        pmh = at("pmh", [P, 2, TOK], F32R)
        CW = SEQ + 2 * CPAD
        hpad = at("hpad", [P, 2, NB, CW], F32)
        o_cl = here()
        cv = at("cv", [P, 2, TOK], F32)
        cvl = at("cvl", [P, 2, TOK], F32R, o_cl)
        o_cvh = here()
        cvh = at("cvh", [P, 2, TOK], F32R)
        assert here() <= nc.sbuf_usable_end, here()
        xs = at("xs", [P, 4, SEQ], F32, o_s)
        hh = at("hh", [P, FT, TOK], F32R, o_m)
        hl = at("hl", [P, FT, TOK], F32R, o_m + FT * 2048)
        fb = at("fb", [P, 3, TOK], F32, o_m + 2 * FT * 2048)
        assert o_m + 2 * FT * 2048 + 6144 <= o_cvh
        top[0] = o_m
        ring = at("ring", [P, ERING, DCH], F32)
        lg = at("lg", [P, TT, NE], F32)
        mx8 = at("mx8", [P, TT, NE], F32)
        ix8 = at("ix8", [P, TT, NE], U32)
        ixf = at("ixf", [P, TT, NE], F32)
        pick = at("pick", [P, 2, TT, NE], F32)
        both = at("both", [P, TT, NE], F32)
        mixk = at("mixk", [P, 2, TT], F32)
        etmp = at("etmp", [P, 4, TT], F32)
        pos = at("pos", [P, TT, NE], F32)
        cnt = at("cnt", [P, NE], F32)
        small = at("small", [P, 8, NE], F32)
        row = at("row", [P, TT, NE], F32)
        rtmp = at("rtmp", [P, TT, NE], F32)
        rowk = at("rowk", [P, 2, TT], F32)
        ridx = at("ridx", [P, 2, TT], U32)
        tabf = at("tabf", [P, 32], F32)
        tab = at("tab", [P, 32], I32)
        t48 = at("t48", [P, 4, NE], F32)
        wcls = at("wcls", [P, 2, MAX_ITEMS + 1], F32)
        slot_no = at("slot_no", [P, CAP], F32)
        sel = at("sel", [P, TT, CAP], F32R)
        ones16 = at("ones16", [P, 2, P], BF16)
        both16 = at("both16", [P, TT, NE], BF16)
        assert here() <= nc.sbuf_usable_end
        top[0] = o_xth + KD * TOK * 4
        rows = at("rows", [P, 2, D], F32)
        xg = at("xg", [P, KD, CAP], F32)
        eh = at("eh", [P, FET, CAP], F32)
        eb = at("eb", [P, 3, CAP], F32)
        assert here() <= o_m, (here(), o_m)
        o = o_m - 2 * TT * D * 4
        assert o >= o_xth + KD * TOK * 4 + 2 * D * 4 * 2
        xrh = at("xrh", [P, TT, D], F32R, o)
        xrl = at("xrl", [P, TT, D], F32R, o + TT * D * 4)
        yt = at("yt", [P, KD, CAP], F32, o_xth)
        yrows = at("yrows", [P, 2, D], F32, o_xth + 8192)
        yg = at("yg", [P, 2, TT, D], F32, o_m)
        zero = at("zero", [P, D], F32, o_cvh)

        bank = [ctx.enter_context(nc.psum_tensor(f"bank{i}", [P, 512], F32)) for i in range(8)]

        in_x = [sem(f"in_x{b}") for b in range(NB)]
        in_cst = sem("in_cst")
        in_slots = sem("in_slots")
        rt_sel = sem("rt_sel")
        xr_hi, xr_lo = sem("xr_hi"), sem("xr_lo")
        x_affine_v = sem("x_affine_v")
        in_small = sem("in_small")
        in_ln = sem("in_ln")
        in_ring = [sem(f"in_raw{i}") for i in range(RAW)]
        hi_done, lo_done, pe_chunk = sem("hi_done"), sem("lo_done"), sem("pe_chunk")
        act_step, dve_step, pool_step = sem("act_step"), sem("dve_step"), sem("pool_step")
        setup_done = sem("setup_done")
        ln_mv, ln_sd, ln_norm = sem("ln_mv"), sem("ln_sd"), sem("ln_norm")
        xt_tr, xs_full, xt_hi, xt_lo = sem("xt_tr"), sem("xs_full"), sem("xt_hi"), sem("xt_lo")
        x_affine = sem("x_affine")
        rows_mm = sem("rows_mm")
        proj_evac = sem("proj_evac")
        rms_ms, rms_sd, roped = sem("rms_ms"), sem("rms_sd"), sem("roped")
        v_tr, v_tok = sem("v_tr"), sem("v_tok")
        pads = sem("pads")
        pool_in, pool_mm, pool_hi, pool_lo = sem("pool_in"), sem("pool_mm"), sem("pool_hi"), sem("pool_lo")
        conv_done, conv_mean, conv_cent = sem("conv_done"), sem("conv_mean"), sem("conv_cent")
        conv_sq, conv_var, conv_sd, conv_nrm, conv_z, conv_act, conv_hi, conv_lo = (
            sem("conv_sq"), sem("conv_var"), sem("conv_sd"), sem("conv_nrm"), sem("conv_z"), sem("conv_act"),
            sem("conv_hi"), sem("conv_lo"))
        sc_mm, sc_max, sc_exp, sc_norm = sem("sc_mm"), sem("sc_max"), sem("sc_exp"), sem("sc_norm")
        p_tr, p_ta, p_tb = sem("p_tr"), sem("p_ta"), sem("p_tb")
        pv_mm, att_full, att_hi, att_lo = sem("pv_mm"), sem("att_full"), sem("att_hi"), sem("att_lo")
        br_gated, br_sum, mg_hi, mg_lo = sem("br_gated"), sem("br_sum"), sem("mg_hi"), sem("mg_lo")
        final_step = sem("final_step")
        ff_th, ff_h, ff_hi, ff_lo = sem("ff_th"), sem("ff_h"), sem("ff_hi"), sem("ff_lo")
        xt_full_a, xt_full_b = sem("xt_full_a"), sem("xt_full_b")
        rt_row = sem("rt_row")
        x_scaled = sem("x_scaled")
        out_norm, out_pool = sem("out_norm"), sem("out_pool")
        zeroed, rt_logit, rt_both, rt_cnt, rt_e, rt_tab = (sem("zeroed"), sem("rt_logit"), sem("rt_both"),
                                                          sem("rt_cnt"), sem("rt_e"), sem("rt_tab"))
        rt_d = sem("rt_d")
        rt_mix = sem("rt_mix")
        zero_set = sem("zero_set")
        scattered = sem("scattered")
        rows_in, rows_tr, xg_a, xg_b = sem("rows_in"), sem("rows_tr"), sem("xg_a"), sem("xg_b")
        in_e = [sem(f"in_e{i}") for i in range(ERING)]
        e_used = sem("e_used")
        e_th, e_h, e_yt, e_ytr, e_yr, e_out = (sem("e_th"), sem("e_h"), sem("e_yt"), sem("e_ytr"), sem("e_yr"),
                                               sem("e_out"))
        all_stored = sem("all_stored")
        gathered = [sem(f"gathered{tt}") for tt in range(TT)]
        out_done = sem("out_done")
        y_ready = sem("y_ready")

        ident = cst[:, C_ID:C_ID + P]
        zero2 = zero[:, :].unsqueeze(1).broadcast_to([P, 2, D])
        cos2 = cst[:, C_COS:C_COS + SEQ].unsqueeze(1).broadcast_to([P, NB, SEQ])
        sin2 = cst[:, C_SIN:C_SIN + SEQ].unsqueeze(1).broadcast_to([P, NB, SEQ])

        def halves(ap):
            return ap.rearrange("p (b t) -> p b t", b=NB)

        def vcol(layer, c):
            return vec[:, layer, c:c + 1]

        xt_banks = ((0, 1, 2, 3, 4, 5, 6, 7), (6, 7, 0, 1, 2, 3, 4, 5), (4, 5, 6, 7, 0, 1, 2, 3),
                    (6, 7, 0, 1, 2, 3, 4, 5))

        def xt_bank(n, h, k):
            return bank[xt_banks[n][4 * h + k // 2]][:, (k % 2) * SEQ:(k % 2 + 1) * SEQ]

        def n_tr(n, h, k):
            return 8 * n + 4 * h + k // 2 + 1

        def n_lo(n, h=1, k=KD - 1):
            return 16 * n + KD * h + k + 1

        def n_hi(n, h, k):
            return 8 * n + 4 * h + k // 2 + 1

        def out_bank(c, tt, per):
            if per == N_OUT // 2:
                return (6, 7, 0, 1, 2, 3, 4, 5)[TT * c + tt]
            return (4, 5, 6, 7, 0, 1, 2, 3)[TT * c + tt]


        block = ctx.enter_context(nc.Block())

        @block.sync
        def _(sp):
            sp.dma_start(cst[:, C_ID:C_ID + P], consts[:, C_ID:C_ID + P]).then_inc(in_cst, 16)
            for b, src in ((0, x0), (1, x1)):
                sp.dma_start(X[:, 2 * b:2 * b + 2, :], src.rearrange("o (t p) d -> p (o t) d", p=P)
                             ).then_inc(in_x[b], 16)
            for g in range(RAW):
                sp.dma_start(raw[:, g, :], dense_w[g]).then_inc(in_ring[g], 16)
                if g == 0:
                    sp.dma_start(cst[:, C_BLK:], consts[:, C_BLK:]).then_inc(in_small, 16)
            sp.dma_start(vec[:, :, :], vecs).then_inc(in_small, 16)
            sp.dma_start(mixw[:, :, :, :], mix).then_inc(in_small, 16)
            sp.dma_start(wrt[:, :, :], wr.rearrange("o (k p) e -> p (o k) e", p=P)).then_inc(in_small, 16)
            sp.dma_start(brt[:, :], br.broadcast_to([P, NE])).then_inc(in_small, 16)

            def ln_rows(n):
                if n == 3:
                    sp.wait_ge(x_affine_v, 2)
                    sp.wait_ge(x_affine, 2 * TT + 2)
                elif n > 0:
                    sp.wait_ge(x_affine, TT * n)
                sp.dma_start(lngb[:, :, :], lnrow[n:n + 1].broadcast_to([P, 2, D])).then_inc(in_ln, 16)

            ln_at = {LAYER_BASE[0] + 40: 0, LAYER_BASE[0] + 100: 1, LAYER_BASE[1] + 40: 2}
            for g in range(RAW, N_DENSE):
                sp.wait_ge(lo_done, g - RAW + 1)
                sp.dma_start(raw[:, g % RAW, :], dense_w[g]).then_inc(in_ring[g % RAW], 16)
                if g in ln_at:
                    ln_rows(ln_at[g])
            sp.wait_ge(mg_lo, 2 * KD)

            def expert_chunk(e, k):
                if k < 2 * FET:
                    src = expert_gu[bass.ds(e * (2 * FET) + k, 1)].rearrange("o p n -> (o p) n")
                    dst = ring[:, k % ERING, 0:CH]
                else:
                    src = expert_dn[bass.ds(e * KD + (k - 2 * FET), 1)].rearrange("o p n -> (o p) n")
                    dst = ring[:, k % ERING, 0:DCH]
                sp.dma_start(dst, src).then_inc(in_e[k % ERING], 16)

            for k in range(ECH):
                if k >= ERING:
                    sp.wait_ge(e_used, k - ERING + 1)
                expert_chunk(0, k)
                if k == ERING - 1:
                    sp.dma_start(slot_no[:, :], slots).then_inc(in_slots, 16)
                    ln_rows(3)
            sp.wait_ge(rt_tab, 1)
            turns = sp.value_load(tab[0:1, 24:25], min_val=NE, max_val=MAX_ITEMS)
            with sp.Fori(1, turns) as j:
                e = sp.value_load(tab[0:1, bass.ds(j, 1)], min_val=0, max_val=NE - 1)
                for k in range(ECH):
                    sp.wait_ge(e_used, j * ECH + (k - ERING + 1))
                    expert_chunk(e, k)
            for tt in range(TT):
                if tt < TT - 1:
                    sp.wait_ge(out_pool, tt + 1)
                else:
                    sp.wait_ge(y_ready, 1)
                dst = (y0, y1)[tt // 2]
                sp.dma_start(dst[0, (tt % 2) * P:(tt % 2 + 1) * P, :], X[:, tt, :]).then_inc(out_done, 16)
            sp.wait_ge(out_done, 16 * TT)

        @block.scalar
        def _(act):
            step = Step(act, act_step)

            def split(g):
                if g >= N_DENSE:
                    return
                act.wait_ge(in_ring[g % RAW], 16 * (g // RAW + 1))
                if g >= SPL:
                    act.wait_ge(pe_chunk, g - SPL + 1)
                nc.scalar.activation(whi[:, g % SPL, :], raw[:, g % RAW, :], ACT.Copy).then_inc(hi_done, 1)

            def ln_sqrt(n):
                for tt in range(TT):
                    act.wait_ge(ln_mv, TT * n + tt + 1)
                    nc.scalar.activation(rstd[:, tt:tt + 1], mv[:, tt, 1:2], ACT.Sqrt,
                                         bias=eps[:, 0:1]).then_inc(ln_sd, 1)

            def xt_evac(n, layer, gcol, bcol):
                for h in range(2):
                    if n == 0 and h == 1:
                        split(0)
                    for k in range(KD):
                        act.wait_ge(xt_tr, n_tr(n, h, k))
                        src, cols, i = xt_bank(n, h, k), slice(h * SEQ, (h + 1) * SEQ), KD * h + k
                        gain, bias = vcol(layer, gcol + k), vcol(layer, bcol + k)
                        if n == 3:
                            if k // 2 % 2 == 0:
                                nc.scalar.activation(xt32[:, k, cols], src, ACT.Identity, scale=gain,
                                                     bias=bias).then_inc(xt_full_a, 1)
                            continue
                        if i >= 4:
                            act.wait_ge(xt_lo, 16 * n + i - 3)
                        if n == 0:
                            nc.scalar.activation(xs[:, i % 4, :], src, ACT.Copy).then_inc(xs_full, 1)
                        else:
                            nc.scalar.activation(xs[:, i % 4, :], src, ACT.Identity, scale=gain,
                                                 bias=bias).then_inc(xs_full, 1)
                        if k % 2 == 0:
                            act.wait_ge(xs_full, 16 * n + i + 1)
                            nc.scalar.activation(xth[:, k, cols], xs[:, i % 4, :], ACT.Copy).then_inc(xt_hi, 1)

            def proj_out(L, m):
                act.wait_ge(pe_chunk, LAYER_BASE[L] + m + 1)
                src = bank[m % 3]
                if m <= 4:
                    nc.scalar.activation(qk[:, m, :], src[:, :], ACT.Copy)
                    if m >= 2:
                        act.wait_ge(rms_ms, 5 * L + m - 1)
                    last = nc.scalar.activation(sq[:, m % 2, :], src[:, :], ACT.Square)
                elif m == M_V:
                    last = nc.scalar.activation(vt[:, :], src[:, :], ACT.Copy)
                elif m < M_CA:
                    act.wait_ge(pads, L + 1)
                    last = nc.scalar.activation(upad[:, m - M_POOL, :, PPAD:PPAD + SEQ], halves(src[:, :]), ACT.Copy)
                elif m < M_CB:
                    last = nc.scalar.activation(hpad[:, m - M_CA, :, CPAD:CPAD + SEQ], halves(src[:, :]), ACT.Copy,
                                                scale=0.5)
                elif m < M_GATE:
                    last = nc.scalar.activation(glu[:, m - M_CB, :], src[:, :], ACT.Tanh, scale=0.5)
                else:
                    last = nc.scalar.activation(gates[:, m - M_GATE, :], src[:, :], ACT.Tanh, scale=0.5,
                                                bias=hvec[:, L, m - M_GATE:m - M_GATE + 1])
                last.then_inc(proj_evac, 1)

            def side(L, m):
                if 2 <= m <= 6:
                    i = m - 2
                    act.wait_ge(rms_ms, 5 * L + i + 1)
                    if i >= 2:
                        act.wait_ge(roped, 5 * L + i - 1)
                    nc.scalar.activation(rms[:, i % 2, :], bank[3 + i % 2][:, :], ACT.Sqrt,
                                         bias=eps[:, 1:2]).then_inc(rms_sd, 1)
                if m == 8:
                    act.wait_ge(v_tr, L + 1)
                    nc.scalar.activation(vtok[:, :, :], bank[5][:, :].rearrange("p (t n) -> p t n", t=TT),
                                         ACT.Copy).then_inc(v_tok, 1)
                s = m - M_GATE
                if s == 2:
                    for ti in range(2):
                        act.wait_ge(pool_mm, 2 * L + ti + 1)
                        step(nc.scalar.activation(pm32[:, ti, :], bank[5 + ti][:, :], ACT.Copy,
                                                  scale=hvec[:, L, 24 + ti:25 + ti]))
                        nc.scalar.activation(pmh[:, ti, :], pm32[:, ti, :], ACT.Copy).then_inc(pool_hi, 1)
                if s >= 3 and s % 2 == 1 and s // 2 - 1 < 8:
                    u = s // 2 - 1
                    act.wait_ge(p_tr, 8 * L + u + 1)
                    if u >= 1:
                        act.wait_ge(pv_mm, 8 * L + u)
                    nc.scalar.activation(probt[:, 0], bank[5][:, :].rearrange("p (s q) -> p s q", s=2),
                                         ACT.Copy).then_inc(p_ta, 1)
                if s >= 1 and s % 2 == 1 and s // 2 < 8:
                    u = s // 2
                    act.wait_ge(sc_max, 8 * L + u + 1)
                    if u >= 1:
                        act.wait_ge(p_tr, 8 * L + u)
                    for q in range(4):
                        a, qt = q // 2, q % 2
                        last = nc.scalar.activation(prob[:, q, :], bank[3 + a][:, qt * SEQ:(qt + 1) * SEQ], ACT.Exp,
                                                    bias=smx[:, 1, q:q + 1], scale=HD ** -0.5,
                                                    accum_out=smx[:, 2, q:q + 1])
                    last.then_inc(sc_exp, 1)
                if s >= 4 and s % 2 == 0 and s // 2 - 2 < 8:
                    u = s // 2 - 2
                    b, mt = u // 4, u % 4
                    act.wait_ge(pv_mm, 8 * L + u + 1)
                    cols = slice(b * SEQ, (b + 1) * SEQ)
                    nc.scalar.activation(att32[:, mt, cols], bank[7][:, 0:SEQ], ACT.Copy,
                                         scale=0.5).then_inc(att_full, 1)
                    act.wait_ge(att_full, 8 * L + u + 1)
                    nc.scalar.activation(atth[:, mt, cols], att32[:, mt, cols], ACT.Copy).then_inc(att_hi, 1)
                if s == 19:
                    act.wait_ge(conv_cent, 2 * L + 2)
                    for ti in range(2):
                        last = nc.scalar.activation(csq[:, ti, :], cv[:, ti, :], ACT.Square)
                    last.then_inc(conv_sq, 1)
                if s == 21:
                    act.wait_ge(conv_var, L + 1)
                    nc.scalar.activation(crs[:, 0, :], bank[4][:, :], ACT.Sqrt, bias=eps[:, 0:1]).then_inc(conv_sd, 1)
                if s == 22:
                    for ti in range(2):
                        act.wait_ge(conv_nrm, 2 * L + ti + 1)
                        step(nc.scalar.activation(cv[:, ti, :], cv[:, ti, :], ACT.Identity,
                                                  scale=hvec[:, L, 26 + ti:27 + ti], bias=hvec[:, L, 28 + ti:29 + ti]))
                        nc.scalar.activation(csq[:, ti, :], cv[:, ti, :], ACT.Tanh, scale=2.0).then_inc(conv_z, 1)
                if s == 23:
                    if L == 1:
                        act.wait_ge(e_out, 16)
                    for ti in range(2):
                        act.wait_ge(conv_act, 2 * L + ti + 1)
                        nc.scalar.activation(cvh[:, ti, :], cv[:, ti, :], ACT.Copy).then_inc(conv_hi, 1)

            xt_evac(0, 0, 0, 0)
            split(1)
            act.wait_ge(in_small, 80)
            act.wait_ge(setup_done, 1)
            for L in range(DEPTH):
                base = LAYER_BASE[L]
                for m in range(N_PROJ):
                    split(base + m + 2)
                    side(L, m)
                    proj_out(L, m)
                def merged_high(j, L=L):
                    act.wait_ge(br_sum, KD * L + j + 1)
                    nc.scalar.activation(xth[:, j, :], mrg[:, j % 2, 0, :], ACT.Copy).then_inc(mg_hi, 1)

                for j in range(N_BR):
                    split(base + N_PROJ + j + 2)
                    if j >= 1:
                        merged_high(j - 1)
                merged_high(KD - 1)
                for j in range(N_OUT - 1):
                    split(base + N_PROJ + N_BR + j + 2)
                ln_sqrt(2 * L)
                xt_evac(2 * L + 1, L, V_L1G, V_L1B)
                if L == 1:
                    break
                g0 = base + N_PROJ + N_BR + N_OUT
                split(g0 + 1)
                for f in range(FT):
                    if f == FT // 2:
                        act.wait_ge(zero_set, 1)
                        act.dma_start(yd[NE * CAP:(NE + 1) * CAP].rearrange("(p s) d -> p s d", p=P), zero2
                                      ).then_inc(e_out, 16)
                    split(g0 + 2 * f + 2)
                    act.wait_ge(pe_chunk, g0 + 2 * f + 1)
                    if f >= 3:
                        act.wait_ge(ff_lo, f - 2)
                    nc.scalar.activation(fb[:, f % 3, :], bank[2 * (f % 2)][:, :], ACT.Tanh,
                                         scale=0.5).then_inc(ff_th, 1)
                    split(g0 + 2 * f + 3)
                    act.wait_ge(ff_h, f + 1)
                    nc.scalar.activation(hh[:, f, :], fb[:, f % 3, :], ACT.Copy).then_inc(ff_hi, 1)
                for k in range(N_DN - 1):
                    split(g0 + N_GU + k + 2)
                ln_sqrt(1)
                xt_evac(2, L, V_L2G, V_L2B)
                split(LAYER_BASE[1] + 1)
            for tt in range(TT):
                if tt < 2:
                    act.wait_ge(x_affine, 2 * TT + tt + 1)
                else:
                    act.wait_ge(x_affine_v, tt - 1)
                nc.scalar.activation(xrh[:, tt, :], X[:, tt, :], ACT.Copy).then_inc(xr_hi, 1)
            act.wait_ge(rt_d, 1)
            nc.scalar.activation(etmp[:, 1, :], etmp[:, 0, :], ACT.Exp).then_inc(rt_e, 1)

            def load_rows(j):
                act.dma_start(rows[:, :, :], xd[bass.ds(j * CAP, CAP)].rearrange("(s p) d -> p s d", p=P)
                              ).then_inc(rows_in, 16)

            def store_rows(j):
                act.dma_start(yd[bass.ds(j * CAP, CAP)].rearrange("(s p) d -> p s d", p=P), yrows[:, :, :]
                              ).then_inc(e_out, 16)

            def xg_evac():
                for q in range(2):
                    act.wait_ge(rows_tr, 2 * q + 1)
                    nc.scalar.activation(xg[:, 4 * q:4 * q + 2, :], bank[4 + 2 * q][:, :].rearrange(
                        "p (k n) -> p k n", k=2), ACT.Copy).then_inc(xg_a, 1)

            xg_evac()
            act.wait_ge(rt_tab, 1)
            turns = act.value_load(tab[0:1, 24:25], min_val=NE, max_val=MAX_ITEMS)
            with act.Fori(0, turns) as j:
                act.wait_ge(rows_tr, 4 * j + 4)
                for f in range(FET):
                    if f == FET // 2:
                        act.wait_ge(scattered, 16 * 2 * TT)
                        load_rows(j + 1)
                    act.wait_ge(e_used, j * ECH + 2 * (f + 1))
                    if f >= 3:
                        act.wait_ge(e_h, j * FET + (f - 2))
                    nc.scalar.activation(eb[:, f % 3, :], bank[f % 3][:, 0:CAP], ACT.Tanh, scale=0.5).then_inc(e_th, 1)
                for q in range(2):
                    act.wait_ge(rows_tr, 4 * j + (4 + 2 * q + 1))
                    nc.scalar.activation(xg[:, 4 * q:4 * q + 2, :], bank[4 + 2 * q][:, :].rearrange(
                        "p (k n) -> p k n", k=2), ACT.Copy).then_inc(xg_a, 1)
                for d in range(KD):
                    act.wait_ge(e_used, j * ECH + (2 * FET + d + 1))
                    nc.scalar.activation(yt[:, d, :], bank[d % 2][:, 0:CAP], ACT.Copy).then_inc(e_yt, 1)
                act.wait_ge(e_yr, j * KD + (KD + 1))
                store_rows(j)
            act.wait_ge(e_out, turns * 16 + 16)
            act.sem_inc(all_stored, 1)
            for tt in range(TT):
                act.wait_ge(ln_mv, 3 * TT + tt + 1)
                nc.scalar.activation(rstd[:, tt:tt + 1], mv[:, tt, 1:2], ACT.Sqrt,
                                     bias=eps[:, 0:1]).then_inc(ln_sd, 1)
                if tt < TT - 1:
                    act.wait_ge(out_norm, tt + 1)
                    nc.scalar.activation(X[:, tt, :], X[:, tt, :], ACT.Identity, scale=rstd[:, tt:tt + 1],
                                         bias=nmr[:, tt:tt + 1]).then_inc(ln_norm, 1)

        @block.vector
        def _(dve):
            step = Step(dve, dve_step)
            V = nc.vector

            def lo(g):
                if g >= N_DENSE:
                    return
                dve.wait_ge(hi_done, g + 1)
                V.tensor_tensor(wlo[:, g % SPL, :], raw[:, g % RAW, :], whi[:, g % SPL, :],
                                ALU.subtract).then_inc(lo_done, 1)

            def xt_low(n):
                for h in range(2):
                    if n == 0 and h == 1:
                        lo(0)
                    for k in range(KD):
                        cols, i = slice(h * SEQ, (h + 1) * SEQ), KD * h + k
                        src = xs[:, i % 4, :]
                        if k % 2 == 1:
                            dve.wait_ge(xs_full, 16 * n + i + 1)
                            step(V.tensor_copy(xth[:, k, cols], src))
                        else:
                            dve.wait_ge(xt_hi, n_hi(n, h, k))
                        V.tensor_tensor(xtl[:, k, cols], src, xth[:, k, cols], ALU.subtract).then_inc(xt_lo, 1)

            def out_rows(n, base, per, n_first):
                for i in range(per):
                    lo(base + i + 2)
                dve.wait_ge(pe_chunk, base + per)
                if n_first:
                    dve.wait_ge(x_affine, n_first)

                def residual(c, tt):
                    cols = slice(c * 512, (c + 1) * 512)
                    return V.scalar_tensor_tensor(X[:, tt, cols], X[:, tt, cols], ALPHA,
                                                  bank[out_bank(c, tt, per)][:, :], ALU.mult, ALU.add)

                for tt in range(TT):
                    ins = residual(0, tt)
                step(ins)
                lo(base + per + 2)
                for tt in range(TT):
                    ins = V.bn_stats(stats[:, tt, 0, :], X[:, tt, 0:512])
                step(ins)
                for i in range(1, per - 1):
                    lo(base + per + i + 2)
                for tt in range(TT):
                    if tt < TT - 1:
                        dve.wait_ge(rows_mm, (TT - 1) * n + tt + 1)
                    else:
                        dve.wait_ge(pe_chunk, base + 2 * per)
                    step(residual(1, tt))
                    step(V.bn_stats(stats[:, tt, 1, :], X[:, tt, 512:1024]))
                    V.bn_aggr(mv[:, tt, :], stats[:, tt, :, :]).then_inc(ln_mv, 1)
                    dve.wait_ge(ln_sd, TT * n + tt + 1)
                    step(V.reciprocal(rstd[:, tt:tt + 1], rstd[:, tt:tt + 1]))
                    V.tensor_scalar(X[:, tt, :], X[:, tt, :], mv[:, tt, 0:1], rstd[:, tt:tt + 1],
                                    ALU.subtract, ALU.mult).then_inc(ln_norm, 1)

            def rope(L, i):
                dve.wait_ge(rms_sd, 5 * L + i + 1)
                g = vcol(L, V_KG if i == 4 else V_QG)
                r, x = rms[:, i % 2, :], qk[:, i, :]
                step(V.reciprocal(r, r))
                step(V.scalar_tensor_tensor(x, x, g, r, ALU.mult, ALU.mult))
                step(V.stream_shuffle(shuf[:, 0, :], x, [(q + 16) % 32 for q in range(32)]))
                V.tensor_tensor(halves(x), halves(x), cos2, ALU.mult)
                step(V.tensor_tensor(halves(shuf[:, 0, :]), halves(shuf[:, 0, :]), sin2, ALU.mult))
                V.tensor_tensor(x, x, shuf[:, 0, :], ALU.add).then_inc(roped, 1)

            def taps(L):
                for k in range(CK):
                    for ti in range(2):
                        src = hpad[:, ti, :, k:k + SEQ]
                        acc = halves(cv[:, ti, :])
                        w = vec[:, L, V_DW + ti * CK + k:V_DW + ti * CK + k + 1]
                        if k == 0:
                            step(V.tensor_scalar(acc, src, w, vcol(L, V_BDW + ti), ALU.mult, ALU.add))
                        else:
                            ins = V.scalar_tensor_tensor(acc, src, w, acc, ALU.mult, ALU.add)
                            if k == CK - 1:
                                ins.then_inc(conv_done, 1)
                            else:
                                step(ins)
                        yield

            def side(L, m, tap):
                if m in ROPE_AT:
                    rope(L, ROPE_AT.index(m))
                if m in (11, 12):
                    ti = m - 11
                    dve.wait_ge(proj_evac, N_PROJ * L + m)
                    x = hpad[:, ti, :, CPAD:CPAD + SEQ]
                    step(V.scalar_tensor_tensor(x, halves(glu[:, ti, :]), 1.0, x, ALU.add, ALU.mult))
                s = m - M_GATE
                if s >= 3 and s % 2 == 1 and s // 2 - 1 < 8:
                    u = s // 2 - 1
                    dve.wait_ge(p_tr, 8 * L + u + 1)
                    if u >= 1:
                        dve.wait_ge(pv_mm, 8 * L + u)
                    V.tensor_copy(probt[:, 1], bank[6][:, :].rearrange("p (s q) -> p s q", s=2)).then_inc(p_tb, 1)
                if s >= 1 and s % 2 == 1 and s // 2 < 8:
                    u = s // 2
                    dve.wait_ge(sc_mm, 8 * L + u + 1)
                    for a in range(2):
                        ins = V.tensor_reduce(smx[:, 0, 2 * a:2 * a + 2],
                                              bank[3 + a][:, :].rearrange("p (q s) -> p q s", q=2), AX.X, ALU.max)
                    step(ins)
                    V.tensor_scalar(smx[:, 1, :], smx[:, 0, :], -HD ** -0.5, None, ALU.mult).then_inc(sc_max, 1)
                if s >= 1:
                    for _i in range(3 if s % 2 else 5):
                        next(tap, None)
                if s >= 1 and s % 2 == 1 and s // 2 < 8:
                    u = s // 2
                    dve.wait_ge(sc_exp, 8 * L + u + 1)
                    step(V.reciprocal(smx[:, 3, :], smx[:, 2, :]))
                    for q in range(4):
                        ins = V.tensor_scalar(prob[:, q, :], prob[:, q, :], smx[:, 3, q:q + 1], None, ALU.mult)
                    ins.then_inc(sc_norm, 1)
                if s == 2:
                    for ti in range(2):
                        dve.wait_ge(pool_hi, 2 * L + ti + 1)
                        V.tensor_tensor(pml[:, ti, :], pm32[:, ti, :], pmh[:, ti, :], ALU.subtract).then_inc(pool_lo, 1)
                if s >= 4 and s % 2 == 0 and s // 2 - 2 < 8:
                    u = s // 2 - 2
                    b, mt = u // 4, u % 4
                    cols = slice(b * SEQ, (b + 1) * SEQ)
                    dve.wait_ge(att_hi, 8 * L + u + 1)
                    V.tensor_tensor(attl[:, mt, cols], att32[:, mt, cols], atth[:, mt, cols],
                                    ALU.subtract).then_inc(att_lo, 1)
                if s == 19:
                    dve.wait_ge(conv_mean, L + 1)
                    for ti in range(2):
                        V.tensor_tensor(cv[:, ti, :], cv[:, ti, :], bank[3][:, :], ALU.subtract).then_inc(conv_cent, 1)
                if s == 21:
                    dve.wait_ge(conv_sd, L + 1)
                    step(V.reciprocal(crs[:, 1, :], crs[:, 0, :]))
                    for ti in range(2):
                        V.tensor_tensor(cv[:, ti, :], cv[:, ti, :], crs[:, 1, :], ALU.mult).then_inc(conv_nrm, 1)
                if s == 22:
                    for ti in range(2):
                        dve.wait_ge(conv_z, 2 * L + ti + 1)
                        V.scalar_tensor_tensor(cv[:, ti, :], csq[:, ti, :], 1.0, cv[:, ti, :], ALU.add,
                                               ALU.mult).then_inc(conv_act, 1)

            V.memset(eps[:, 0:1], LN_EPS)
            V.memset(eps[:, 1:2], RMS_EPS)
            xt_low(0)
            lo(1)
            dve.wait_ge(in_small, 80)
            for L in range(DEPTH):
                V.tensor_scalar(hvec[:, L, 0:26], vec[:, L, V_BG:V_BG + 26], 0.5, None, ALU.mult)
                step(V.tensor_scalar(hvec[:, L, 26:30], vec[:, L, V_CG:V_CG + 4], 0.25, None, ALU.mult))
            V.tensor_scalar(hvec[:, :, 30:32], hvec[:, :, 0:2], 1.0, None, ALU.mult).then_inc(setup_done, 1)
            for L in range(DEPTH):
                base = LAYER_BASE[L]
                tap = taps(L)
                for m in range(N_PROJ):
                    lo(base + m + 2)
                    side(L, m, tap)
                for ti in range(2):
                    dve.wait_ge(conv_hi, 2 * L + ti + 1)
                    V.tensor_tensor(cvl[:, ti, :], cv[:, ti, :], cvh[:, ti, :], ALU.subtract).then_inc(conv_lo, 1)
                def merged_low(j, L=L):
                    dve.wait_ge(mg_hi, KD * L + j + 1)
                    V.tensor_tensor(xtl[:, j, :], mrg[:, j % 2, 0, :], xth[:, j, :], ALU.subtract).then_inc(mg_lo, 1)

                dve.wait_ge(proj_evac, N_PROJ * (L + 1))
                for j in range(N_BR):
                    lo(base + N_PROJ + j + 2)
                    dve.wait_ge(pe_chunk, base + N_PROJ + j + 1)
                    if j >= 2:
                        dve.wait_ge(mg_lo, KD * L + j - 1)
                    for i in range(3):
                        ins = V.scalar_tensor_tensor(mrg[:, j % 2, i, :], gates[:, 8 * i + j, :], 1.0,
                                                     bank[3 * (j % 2) + i][:, :], ALU.add, ALU.mult)
                    ins.then_inc(br_gated, 1)
                    if j >= 1:
                        merged_low(j - 1)
                merged_low(KD - 1)
                out_rows(2 * L, base + N_PROJ + N_BR, N_OUT // 2, 2 * TT * L)
                if L == 1:
                    break
                xt_low(1)
                lo(base + N_PROJ + N_BR + N_OUT + 1)
                g0 = base + N_PROJ + N_BR + N_OUT
                for f in range(FT):
                    lo(g0 + 2 * f + 2)
                    dve.wait_ge(ff_th, f + 1)
                    b = fb[:, f % 3, :]
                    step(V.scalar_tensor_tensor(b, b, 1.0, bank[2 * (f % 2)][:, :], ALU.add, ALU.mult))
                    lo(g0 + 2 * f + 3)
                    dve.wait_ge(pe_chunk, g0 + 2 * f + 2)
                    V.scalar_tensor_tensor(b, b, 0.5, bank[2 * (f % 2) + 1][:, :], ALU.mult, ALU.mult).then_inc(ff_h, 1)
                    dve.wait_ge(ff_hi, f + 1)
                    V.tensor_tensor(hl[:, f, :], b, hh[:, f, :], ALU.subtract).then_inc(ff_lo, 1)
                out_rows(1, g0 + N_GU, N_DN // 2, TT)
                xt_low(2)
                lo(LAYER_BASE[1] + 1)

            for i, c in enumerate((C_ONE, C_TRI)):
                V.tensor_copy(ones16[:, i, :], cst[:, c:c + P])
            for h in range(2):
                for k in (2, 3, 6, 7):
                    dve.wait_ge(xt_tr, n_tr(3, h, k))
                    V.tensor_scalar(xt32[:, k, h * SEQ:(h + 1) * SEQ], xt_bank(3, h, k), vcol(1, V_L1G + k),
                                    vcol(1, V_L1B + k), ALU.mult, ALU.add).then_inc(xt_full_b, 1)
            dve.wait_ge(in_ln, 16 * 3)
            for tt in (2, 3):
                step(V.tensor_tensor(X[:, tt, :], X[:, tt, :], lngb[:, 0, :], ALU.mult))
                V.tensor_tensor(X[:, tt, :], X[:, tt, :], lngb[:, 1, :], ALU.add).then_inc(x_affine_v, 1)

            def x_low(tt):
                dve.wait_ge(xr_hi, tt + 1)
                V.tensor_tensor(xrl[:, tt, :], X[:, tt, :], xrh[:, tt, :], ALU.subtract).then_inc(xr_lo, 1)

            x_low(0)
            x_low(1)
            dve.wait_ge(rt_logit, 1)
            b0 = bank[0]
            step(V.tensor_tensor(lg[:, :, :], brt[:, :].unsqueeze(1).broadcast_to([P, TT, NE]),
                                 b0[:, 0:TT * NE].rearrange("p (t e) -> p t e", t=TT), ALU.add))
            for tt in range(TT):
                ins = V.max(mx8[:, tt, :], lg[:, tt, :])
            step(ins)
            for tt in range(TT):
                ins = V.max_index(ix8[:, tt, :], mx8[:, tt, :], lg[:, tt, :])
            step(ins)
            step(V.tensor_copy(ixf[:, :, :], ix8[:, :, :]))
            i8 = cst[:, C_I8:C_I8 + 8]
            for k in range(2):
                step(V.tensor_tensor(pick[:, k], i8.unsqueeze(1).broadcast_to([P, TT, NE]),
                                     ixf[:, :, k:k + 1].broadcast_to([P, TT, NE]), ALU.is_equal))
            V.tensor_tensor(both16[:, :, :], pick[:, 0], pick[:, 1], ALU.add).then_inc(rt_both, 1)
            V.tensor_tensor(both[:, :, :], pick[:, 0], pick[:, 1], ALU.add)
            V.tensor_tensor(etmp[:, 0, :], mx8[:, :, 1], mx8[:, :, 0], ALU.subtract).then_inc(rt_d, 1)
            x_low(2)
            x_low(3)
            dve.wait_ge(rt_cnt, 1)
            b1 = bank[1]
            V.tensor_copy(pos[:, :, :], b1[:, 0:TT * NE].rearrange("p (t e) -> p t e", t=TT))
            step(V.tensor_copy(cnt[:, :], b1[:, TT * NE:TT * NE + NE]))
            dve.wait_ge(in_slots, 16)
            for tt in range(TT):
                ins = V.tensor_scalar(sel[:, tt, :], slot_no[:, :], pos[:, tt, 0:1], both[:, tt, 0:1], ALU.is_equal,
                                      ALU.mult)
            ins.then_inc(rt_sel, 1)
            over, cum, before, delta, n0, n1, one = (small[:, i, :] for i in range(7))
            V.memset(one, 1.0)
            V.tensor_scalar(n0, cnt[:, :], float(CAP), None, ALU.min)
            V.tensor_scalar(n1, cnt[:, :], float(-CAP), None, ALU.add)
            step(V.tensor_scalar(over, cnt[:, :], float(CAP), None, ALU.is_gt))
            step(V.tensor_tensor_scan(cum, one, over, 0.0, ALU.mult, ALU.add))
            step(V.tensor_tensor(before, cum, over, ALU.subtract))
            step(V.tensor_scalar(delta, before, float(CAP), float((NE - 1) * CAP), ALU.mult, ALU.add))
            e256 = cst[:, C_E256:C_E256 + 8]
            step(V.tensor_tensor(delta, delta, e256, ALU.subtract))
            step(V.tensor_scalar(row[:, :, :], pos[:, :, :], float(CAP), None, ALU.is_ge))
            step(V.tensor_tensor(row[:, :, :], row[:, :, :], delta.unsqueeze(1).broadcast_to([P, TT, NE]), ALU.mult))
            step(V.tensor_tensor(row[:, :, :], row[:, :, :], pos[:, :, :], ALU.add))
            step(V.tensor_tensor(row[:, :, :], row[:, :, :], e256.unsqueeze(1).broadcast_to([P, TT, NE]), ALU.add))
            for k in range(2):
                step(V.tensor_tensor(rtmp[:, :, :], row[:, :, :], pick[:, k], ALU.mult))
                step(V.tensor_reduce(rowk[:, k, :], rtmp[:, :, :], AX.X, ALU.add))
            V.tensor_copy(ridx[:, :, :], rowk[:, :, :]).then_inc(rt_row, 1)
            step(V.memset(tabf[:, :], 0.0))
            V.tensor_copy(tabf[:, 0:8], i8)
            V.tensor_copy(tabf[:, 12:20], n0)
            V.tensor_scalar(tabf[:, 24:25], cum[:, 7:8], float(NE), None, ALU.add)
            step(V.tensor_tensor(t48[:, :, :], before.unsqueeze(1).broadcast_to([P, 4, NE]),
                                 cst[:, C_I4:C_I4 + 4].unsqueeze(2).broadcast_to([P, 4, NE]), ALU.is_equal))
            step(V.tensor_tensor(t48[:, :, :], t48[:, :, :], over.unsqueeze(1).broadcast_to([P, 4, NE]), ALU.mult))
            for what, dst in ((i8, 8), (n1, 20)):
                step(V.tensor_tensor(rtmp[:, :, :], t48[:, :, :], what.unsqueeze(1).broadcast_to([P, 4, NE]), ALU.mult))
                step(V.tensor_reduce(tabf[:, dst:dst + 4], rtmp[:, :, :], AX.X, ALU.add))
            items = tabf[:, 12:24]
            for i, n in enumerate(WIDTHS[:-1]):
                if i == 0:
                    step(V.tensor_scalar(wcls[:, 0, :], items, float(n), None, ALU.is_gt))
                else:
                    step(V.tensor_scalar(wcls[:, 1, :], items, float(n), None, ALU.is_gt))
                    step(V.tensor_tensor(wcls[:, 0, :], wcls[:, 0, :], wcls[:, 1, :], ALU.add))
            step(V.tensor_copy(items, wcls[:, 0, :]))
            V.tensor_copy(tab[:, :], tabf[:, :]).then_inc(rt_tab, 1)

            dve.wait_ge(rt_e, 1)
            step(V.tensor_scalar(etmp[:, 2, :], etmp[:, 1, :], 1.0, None, ALU.add))
            step(V.reciprocal(mixk[:, 0, :], etmp[:, 2, :]))
            V.tensor_tensor(mixk[:, 1, :], etmp[:, 1, :], mixk[:, 0, :], ALU.mult).then_inc(rt_mix, 1)
            def xg_evac():
                for q in range(2):
                    dve.wait_ge(rows_tr, 2 * q + 2)
                    V.tensor_copy(xg[:, 4 * q + 2:4 * q + 4, :], bank[5 + 2 * q][:, :].rearrange(
                        "p (k n) -> p k n", k=2)).then_inc(xg_b, 1)

            dve.wait_ge(rt_tab, 1)
            turns = dve.value_load(tab[0:1, 24:25], min_val=NE, max_val=MAX_ITEMS)
            xg_evac()
            dve.sem_inc(e_yr, 1)
            t_base = step.n
            with dve.Fori(0, turns) as j:
                step.turn(j * FET + t_base)
                for f in range(FET):
                    dve.wait_ge(e_th, j * FET + (f + 1))
                    b = eb[:, f % 3, :]
                    step(V.scalar_tensor_tensor(b, b, 1.0, bank[f % 3][:, 0:CAP], ALU.add, ALU.mult))
                    V.scalar_tensor_tensor(eh[:, f, :], b, 0.5, bank[f % 3][:, CAP:2 * CAP], ALU.mult,
                                           ALU.mult).then_inc(e_h, 1)
                for q in range(2):
                    dve.wait_ge(rows_tr, 4 * j + (4 + 2 * q + 2))
                    V.tensor_copy(xg[:, 4 * q + 2:4 * q + 4, :], bank[5 + 2 * q][:, :].rearrange(
                        "p (k n) -> p k n", k=2)).then_inc(xg_b, 1)
                for d in range(KD):
                    dve.wait_ge(e_ytr, j * KD + (d + 1))
                    if d == 0:
                        dve.wait_ge(e_out, 16 * j + 16)
                    V.tensor_copy(yrows[:, :, d * P:(d + 1) * P], bank[2 + d % 2][:, 0:2 * P].rearrange(
                        "p (s n) -> p s n", s=2)).then_inc(e_yr, 1)
            fin = Step(dve, final_step)
            dve.wait_ge(rt_mix, 1)
            dve.wait_ge(in_ln, 64)
            gain, bias = lngb[:, 0, :], lngb[:, 1, :]
            for tt in range(TT):
                x, std = X[:, tt, :], rstd[:, tt:tt + 1]
                dve.wait_ge(x_scaled, tt + 1)
                dve.wait_ge(gathered[tt], 32)
                for k in range(2):
                    fin(V.scalar_tensor_tensor(x, yg[:, k, tt, :], mixk[:, k, tt:tt + 1], x, ALU.mult, ALU.add))
                V.bn_stats(stats[:, tt, 0, :], X[:, tt, 0:512])
                fin(V.bn_stats(stats[:, tt, 1, :], X[:, tt, 512:1024]))
                V.bn_aggr(mv[:, tt, :], stats[:, tt, :, :]).then_inc(ln_mv, 1)
                dve.wait_ge(ln_sd, 3 * TT + tt + 1)
                fin(V.reciprocal(std, std))
                if tt < TT - 1:
                    V.scalar_tensor_tensor(nmr[:, tt:tt + 1], mv[:, tt, 0:1], -1.0, std, ALU.mult,
                                           ALU.mult).then_inc(out_norm, 1)
                else:
                    fin(V.scalar_tensor_tensor(x, x, mv[:, tt, 0:1], gain, ALU.subtract, ALU.mult))
                    V.scalar_tensor_tensor(x, x, std, bias, ALU.mult, ALU.add).then_inc(y_ready, 1)

        @block.gpsimd
        def _(pool):
            G = nc.gpsimd
            step = Step(pool, pool_step)

            def zero_fill(L):
                g0 = LAYER_BASE[L] + N_PROJ + N_BR + N_OUT
                pool.wait_ge(pe_chunk, g0)
                G.memset(zero[:, :], 0.0).then_inc(zero_set, 1)
                pool.wait_ge(zero_set, 1)
                parts = [(xd, i) for i in range(N_ROWS // 256)] + [(yd, i) for i in range(NE + 1, N_ROWS // 256)]
                for n, (dst, i) in enumerate(parts):
                    pool.wait_ge(pe_chunk, g0 + 2 + 3 * n)
                    pool.dma_start(dst[i * 256:(i + 1) * 256].rearrange("(p s) d -> p s d", p=P),
                                   zero2).then_inc(zeroed, 16)
                pool.wait_ge(zeroed, 16 * len(parts))

            def affine(n):
                pool.wait_ge(in_ln, 16 * (n + 1))
                for tt in range(TT if n < 2 else 2):
                    pool.wait_ge(xt_tr, n_tr(n + 1, tt // 2, KD - 1))
                    step(G.tensor_tensor(X[:, tt, :], X[:, tt, :], lngb[:, 0, :], ALU.mult))
                    G.tensor_tensor(X[:, tt, :], X[:, tt, :], lngb[:, 1, :], ALU.add).then_inc(x_affine, 1)

            for L in range(DEPTH):
                pool.wait_ge(xt_lo, n_lo(2 * L))
                for lo_, hi_ in ((0, PPAD), (PPAD + SEQ, PW)):
                    G.memset(upad[:, :, :, lo_:hi_], 0.0)
                G.memset(hpad[:, :, :, 0:CPAD], 0.0)
                G.memset(hpad[:, :, :, CPAD + SEQ:CW], 0.0).then_inc(pads, 1)
                if L == 1:
                    affine(1)
                pool.wait_ge(in_small, 80)
                pool.wait_ge(proj_evac, N_PROJ * L + M_CA)
                for ti in range(2):
                    G.tensor_tensor(psa[:, ti, :, 1:PW], upad[:, ti, :, 0:PW - 1], upad[:, ti, :, 1:PW],
                                    ALU.add).then_inc(pool_step, 1)
                step.n += 2
                pool.wait_ge(pool_step, step.n)
                for ti in range(2):
                    G.tensor_tensor(psb[:, ti, :, 2:PW - 1], psa[:, ti, :, 1:PW - 2], psa[:, ti, :, 3:PW],
                                    ALU.add).then_inc(pool_step, 1)
                step.n += 2
                pool.wait_ge(pool_step, step.n)
                step(G.tensor_tensor(psa[:, 1, :, 4:PW - 3], psb[:, 1, :, 2:PW - 5], psb[:, 1, :, 6:PW - 1], ALU.add))
                step(G.tensor_tensor(psb[64:P, 1, :, 8:PW - 8], psa[64:P, 1, :, 4:PW - 12], psa[64:P, 1, :, 12:PW - 4],
                                     ALU.add))
                for ti in range(2):
                    for h in range(2):
                        ps = slice(64 * h, 64 * h + 64)
                        inv = cst[ps, C_INV + ti * SEQ:C_INV + (ti + 1) * SEQ].unsqueeze(1).broadcast_to([64, NB, SEQ])
                        o_ = halves(pooled[ps, ti, :])
                        src = (psa, psb)[h]
                        step(G.tensor_tensor(o_, src[ps, ti, :, PPAD:PPAD + SEQ], inv, ALU.mult))
                        ins = G.tensor_tensor(o_, o_, upad[ps, ti, :, PPAD:PPAD + SEQ], ALU.subtract)
                        if ti == 1 and h == 1:
                            ins.then_inc(pool_in, 1)
                        else:
                            step(ins)
                for j in range(N_BR):
                    pool.wait_ge(br_gated, KD * L + j + 1)
                    m = mrg[:, j % 2]
                    step(G.tensor_tensor(m[:, 0, :], m[:, 0, :], m[:, 1, :], ALU.add))
                    G.tensor_tensor(m[:, 0, :], m[:, 0, :], m[:, 2, :], ALU.add).then_inc(br_sum, 1)
                affine(2 * L)
                if L == 0:
                    zero_fill(L)
            pool.wait_ge(rt_row, 1)
            pool.wait_ge(x_affine, 2 * TT + 2)
            pool.wait_ge(x_affine_v, 2)
            for tt in range(TT):
                for k in range(2):
                    pool.indirect_dma_start(out=xd, out_offset=bass.IndirectOffsetOnAxis(
                        ap=ridx[:, k, tt:tt + 1], axis=0), in_=X[:, tt, :], in_offset=None).then_inc(scattered, 16)
            pool.wait_ge(scattered, 16 * 2 * TT)
            pool.wait_ge(xr_lo, TT)
            for tt in range(TT):
                G.tensor_scalar(X[:, tt, :], X[:, tt, :], ALPHA, None, ALU.mult).then_inc(x_scaled, 1)
            pool.wait_ge(all_stored, 1)
            for tt in range(TT):
                for k in range(2):
                    pool.indirect_dma_start(out=yg[:, k, tt, :], out_offset=None, in_=yd,
                                            in_offset=bass.IndirectOffsetOnAxis(ap=ridx[:, k, tt:tt + 1], axis=0)
                                            ).then_inc(gathered[tt], 16)
            pool.wait_ge(in_ln, 64)
            for tt in range(TT - 1):
                pool.wait_ge(ln_norm, 3 * TT + tt + 1)
                step(G.tensor_tensor(X[:, tt, :], X[:, tt, :], lngb[:, 0, :], ALU.mult))
                G.tensor_tensor(X[:, tt, :], X[:, tt, :], lngb[:, 1, :], ALU.add).then_inc(out_pool, 1)

        @block.tensor
        def _(pe):
            mm = nc.tensor.matmul

            def transposes(n):
                if n == 0:
                    pe.wait_ge(in_cst, 16)
                for h in range(2):
                    if n == 0:
                        pe.wait_ge(in_x[h], 16)
                    else:
                        pe.wait_ge(ln_norm, TT * (n - 1) + 2 * h + 2)
                    for k in range(KD):
                        for t in range(2):
                            last = nc.tensor.transpose(xt_bank(n, h, k)[:, t * P:(t + 1) * P],
                                                       X[:, 2 * h + t, k * P:(k + 1) * P], ident)
                        if k % 2 == 1:
                            last.then_inc(xt_tr, 1)

            def three(out, wh, wl, xh, xl, first, last):
                mm(out, wh, xh, start=first, stop=False)
                mm(out, wh, xl, start=False, stop=False)
                return mm(out, wl, xh, start=False, stop=last)

            def wtile(g, k):
                return whi[:, g % SPL, k * P:(k + 1) * P], wlo[:, g % SPL, k * P:(k + 1) * P]

            def features(g, out, first=None):
                pe.wait_ge(lo_done, g + 1)
                for k in range(KD):
                    if first is not None:
                        pe.wait_ge(xt_lo, n_lo(first, 1, max(k, 1)))
                    wh, wl = wtile(g, k)
                    ins = three(out, wh, wl, xth[:, k, :], xtl[:, k, :], k == 0, k == KD - 1)
                ins.then_inc(pe_chunk, 1)

            def token_rows(base, per, ah, al, ready, branches_read=0):
                def tile(c, i, kk, tt):
                    g, k = base + c * per + i, 2 * i + kk
                    wh = whi[:, g % SPL, kk * 512:(kk + 1) * 512]
                    wl = wlo[:, g % SPL, kk * 512:(kk + 1) * 512]
                    out = bank[out_bank(c, tt, per)][:, :]
                    t = slice(tt * P, (tt + 1) * P)
                    mm(out, ah[:, k, t], wh, start=(k == 0), stop=False)
                    mm(out, ah[:, k, t], wl, start=False, stop=False)
                    return mm(out, al[:, k, t], wh, start=False, stop=(k == 2 * per - 1))

                for c in range(2):
                    if c == 1 and branches_read:
                        pe.wait_ge(br_gated, branches_read)
                    for i in range(per if c == 0 else per - 2):
                        pe.wait_ge(lo_done, base + c * per + i + 1)
                        for kk in range(2):
                            if c == 0:
                                ready(2 * i + kk)
                            for tt in range(TT):
                                ins = tile(c, i, kk, tt)
                        ins.then_inc(pe_chunk, 1)
                pe.wait_ge(lo_done, base + 2 * per)
                for tt in range(TT):
                    for i in (per - 2, per - 1):
                        for kk in range(2):
                            ins = tile(1, i, kk, tt)
                        if tt == TT - 1:
                            ins.then_inc(pe_chunk, 1)
                    if tt < TT - 1:
                        ins.then_inc(rows_mm, 1)

            def side(L, m):
                if 1 <= m <= 5:
                    i = m - 1
                    if m == 1:
                        pe.wait_ge(in_small, 80)
                    pe.wait_ge(proj_evac, N_PROJ * L + i + 1)
                    if i >= 2:
                        pe.wait_ge(rms_sd, 5 * L + i - 1)
                    mm(bank[3 + i % 2][:, :], cst[:, C_BLK:C_BLK + P], sq[:, i % 2, :], start=True,
                       stop=True).then_inc(rms_ms, 1)
                if m == 6:
                    pe.wait_ge(proj_evac, N_PROJ * L + M_V + 1)
                    for tt in range(TT):
                        ins = nc.tensor.transpose(bank[5][:, tt * P:(tt + 1) * P], vt[:, tt * P:(tt + 1) * P], ident)
                    ins.then_inc(v_tr, 1)
                s = m - M_GATE
                if s == 1:
                    pe.wait_ge(pool_in, L + 1)
                    pe.wait_ge(v_tok, L + 1)
                    for ti in range(2):
                        mm(bank[5 + ti][:, :], mixw[:, L, ti, :], pooled[:, ti, :], start=True,
                           stop=True).then_inc(pool_mm, 1)
                if s >= 2 and s % 2 == 0 and s // 2 - 1 < 8:
                    u = s // 2 - 1
                    pe.wait_ge(sc_norm, 8 * L + u + 1)
                    if u == 0:
                        pe.wait_ge(pool_hi, 2 * L + 2)
                    else:
                        pe.wait_ge(p_ta, 8 * L + u)
                        pe.wait_ge(p_tb, 8 * L + u)
                    for a in range(2):
                        for st in range(2):
                            for qt in range(2):
                                o_ = st * SEQ + qt * P
                                ins = nc.tensor.transpose(bank[5 + a][:, o_:o_ + P],
                                                          prob[:, 2 * a + qt, st * P:(st + 1) * P], ident)
                    ins.then_inc(p_tr, 1)
                if s >= 0 and s % 2 == 0 and s // 2 < 8:
                    u = s // 2
                    b, mt = u // 4, u % 4
                    pe.wait_ge(roped, 5 * L + 5)
                    if u == 0:
                        pe.wait_ge(rms_sd, 5 * L + 5)
                    if u >= 1:
                        pe.wait_ge(sc_exp, 8 * L + u)
                    for a in range(2):
                        h = slice(64 * a, 64 * a + 64)
                        for qt in range(2):
                            q0 = b * SEQ + qt * P
                            ins = mm(bank[3 + a][:, qt * SEQ:(qt + 1) * SEQ], qk[h, mt, q0:q0 + P],
                                     qk[h, 4, b * SEQ:(b + 1) * SEQ], start=True, stop=True)
                    ins.then_inc(sc_mm, 1)
                if s >= 3 and s % 2 == 1 and s // 2 - 1 < 8:
                    u = s // 2 - 1
                    b = u // 4
                    pe.wait_ge(p_ta, 8 * L + u + 1)
                    pe.wait_ge(p_tb, 8 * L + u + 1)
                    if u >= 1:
                        pe.wait_ge(att_full, 8 * L + u)
                    for a in range(2):
                        h = slice(64 * a, 64 * a + 64)
                        for st in range(2):
                            ins = mm(bank[7][h, 0:SEQ], vtok[:, 2 * b + st, h], probt[:, a, st, :],
                                     start=(st == 0), stop=(st == 1))
                    ins.then_inc(pv_mm, 1)
                if s == 18:
                    pe.wait_ge(conv_done, 2 * L + 2)
                    for ti in range(2):
                        ins = mm(bank[3][:, :], cst[:, C_MEAN:C_MEAN + P], cv[:, ti, :], start=(ti == 0),
                                 stop=(ti == 1))
                    ins.then_inc(conv_mean, 1)
                if s == 20:
                    pe.wait_ge(conv_sq, L + 1)
                    for ti in range(2):
                        ins = mm(bank[4][:, :], cst[:, C_MEAN:C_MEAN + P], csq[:, ti, :], start=(ti == 0),
                                 stop=(ti == 1))
                    ins.then_inc(conv_var, 1)

            transposes(0)
            for L in range(DEPTH):
                base = LAYER_BASE[L]
                for m in range(N_PROJ):
                    if m >= 3:
                        pe.wait_ge(proj_evac, N_PROJ * L + m - 2)
                    features(base + m, bank[m % 3][:, :], 2 * L if m == 0 else None)
                    side(L, m)
                pe.wait_ge(att_lo, 8 * (L + 1))
                pe.wait_ge(pool_lo, 2 * (L + 1))
                pe.wait_ge(proj_evac, N_PROJ * (L + 1))
                pe.wait_ge(conv_lo, 2 * (L + 1))
                for j in range(N_BR):
                    g = base + N_PROJ + j
                    pe.wait_ge(lo_done, g + 1)
                    if j >= 2:
                        pe.wait_ge(br_gated, KD * L + j - 1)
                    k = 0
                    for i, (ah, al, n) in enumerate(((atth, attl, 4), (pmh, pml, 2), (cvh, cvl, 2))):
                        for t in range(n):
                            wh, wl = wtile(g, k)
                            ins = three(bank[3 * (j % 2) + i][:, :], wh, wl, ah[:, t, :], al[:, t, :], t == 0,
                                        t == n - 1)
                            k += 1
                    ins.then_inc(pe_chunk, 1)
                pe.wait_ge(br_gated, KD * L + KD - 1)
                def merged(k, L=L):
                    pe.wait_ge(mg_lo, KD * L + k + 1)

                token_rows(base + N_PROJ + N_BR, N_OUT // 2, xth, xtl, merged, KD * (L + 1))
                if L == 1:
                    break
                transposes(1)
                g0 = base + N_PROJ + N_BR + N_OUT
                for f in range(FT):
                    if f >= 2:
                        pe.wait_ge(ff_h, f - 1)
                    features(g0 + 2 * f, bank[2 * (f % 2)][:, :], 1 if f == 0 else None)
                    features(g0 + 2 * f + 1, bank[2 * (f % 2) + 1][:, :])

                def hidden(k):
                    pe.wait_ge(ff_lo, k + 1)

                token_rows(g0 + N_GU, N_DN // 2, hh, hl, hidden)
                transposes(2)

            transposes(3)
            for tt in range(TT):
                pe.wait_ge(xt_full_a, 4 * (tt // 2) + 4)
                pe.wait_ge(xt_full_b, 4 * (tt // 2) + 4)
                for k in range(KD):
                    ins = mm(bank[0][:, tt * NE:(tt + 1) * NE], xt32[:, k, tt * P:(tt + 1) * P], wrt[:, k, :],
                             start=(k == 0), stop=(k == KD - 1))
            ins.then_inc(rt_logit, 1)
            pe.wait_ge(rt_both, 1)
            for tt in range(TT):
                for i in range(tt):
                    mm(bank[1][:, tt * NE:(tt + 1) * NE], ones16[:, 0, :], both16[:, i, :], start=(i == 0), stop=False)
                mm(bank[1][:, tt * NE:(tt + 1) * NE], ones16[:, 1, :], both16[:, tt, :], start=(tt == 0), stop=True)
            for i in range(TT):
                ins = mm(bank[1][:, TT * NE:TT * NE + NE], ones16[:, 0, :], both16[:, i, :], start=(i == 0),
                         stop=(i == TT - 1))
            ins.then_inc(rt_cnt, 1)
            pe.wait_ge(xr_lo, TT)
            pe.wait_ge(rt_sel, 1)
            for k in range(KD):
                for tt in range(TT):
                    for part in (xrh, xrl):
                        ins = mm(bank[4 + k // 2][:, (k % 2) * CAP:(k % 2 + 1) * CAP], part[:, tt, k * P:(k + 1) * P],
                                 sel[:, tt, :], start=(tt == 0 and part is xrh), stop=(tt == TT - 1 and part is xrl))
                if k % 2 == 1:
                    ins.then_inc(rows_tr, 1)
            pe.wait_ge(rt_tab, 1)
            turns = pe.value_load(tab[0:1, 24:25], min_val=NE, max_val=MAX_ITEMS)

            def rows_to_features():
                for kp in range(4):
                    for kk in range(2):
                        for st in range(2):
                            o_ = kk * CAP + st * P
                            k = 2 * kp + kk
                            ins = nc.tensor.transpose(bank[4 + kp][:, o_:o_ + P], rows[:, st, k * P:(k + 1) * P], ident)
                    ins.then_inc(rows_tr, 1)

            with pe.Fori(0, turns) as j:
                pe.wait_ge(xg_a, 2 * j + 2)
                pe.wait_ge(xg_b, 2 * j + 2)
                lap = j * (16 * (ECH // ERING))
                width = pe.value_load(tab[0:1, bass.ds(j + 12, 1)], min_val=0, max_val=len(WIDTHS) - 1)

                def back(d):
                    pe.wait_ge(e_yt, j * KD + (d + 1))
                    if d >= 2:
                        pe.wait_ge(e_yr, j * KD + d)
                    for st in range(2):
                        ins = nc.tensor.transpose(bank[2 + d % 2][:, st * P:(st + 1) * P],
                                                  yt[:, d, st * P:(st + 1) * P], ident)
                    ins.then_inc(e_ytr, 1)

                def item(n):
                    for f in range(FET):
                        if f == 2:
                            pe.wait_ge(e_yr, j * KD + 1)
                        if f >= 3:
                            pe.wait_ge(e_h, j * FET + (f - 2))
                        for w in range(2):
                            k = 2 * f + w
                            pe.wait_ge(in_e[k % ERING], lap + 16 * (k // ERING + 1))
                            for t in range(KD):
                                ins = mm(bank[f % 3][:, w * CAP:w * CAP + n], ring[:, k % ERING, t * P:(t + 1) * P],
                                         xg[:, t, 0:n], start=(t == 0), stop=(t == KD - 1))
                            ins.then_inc(e_used, 1)
                    pe.wait_ge(rows_in, 16 * j + 16)
                    rows_to_features()
                    pe.wait_ge(e_h, j * FET + FET)
                    for d in range(KD):
                        k = 2 * FET + d
                        if d >= 2:
                            pe.wait_ge(e_yt, j * KD + (d - 1))
                        pe.wait_ge(in_e[k % ERING], lap + 16 * (k // ERING + 1))
                        for t in range(FET):
                            ins = mm(bank[d % 2][:, 0:n], ring[:, k % ERING, t * P:(t + 1) * P], eh[:, t, 0:n],
                                     start=(t == 0), stop=(t == FET - 1))
                        ins.then_inc(e_used, 1)
                        if d >= 1:
                            back(d - 1)
                    back(KD - 1)

                def among(first, last):
                    if first == last:
                        item(WIDTHS[first])
                        return
                    mid = 0 if first == 0 else (first + last) // 2
                    with pe.If(width <= mid):
                        among(first, mid)
                    with pe.Else():
                        among(mid + 1, last)

                among(0, len(WIDTHS) - 1)


def tiles_by_column(w):
    k, n = w.shape
    return np.ascontiguousarray(w.reshape(k // P, P, n // P, P).transpose(2, 1, 0, 3)).reshape(n // P, P, k)


def rows_by_half(w):
    k = w.shape[0]
    return np.ascontiguousarray(w.reshape(k // 256, 2, P, 2, 512).transpose(3, 0, 2, 1, 4)).reshape(-1, P, CH)


def heads_paired(w, axis):
    order = [h for i in range(4) for h in (i, i + 4)]
    parts = np.split(w, 8, axis=axis)
    return np.concatenate([parts[h] for h in order], axis=axis)


def kernel(**inputs):
    import concourse.bacc as bacc
    from concourse.bass_utils import run_bass_kernel_spmd

    a = {k: np.asarray(v) for k, v in inputs.items()}

    def col(v):
        return np.ascontiguousarray(v.reshape(-1, P).T)

    stream = []
    for L in range(DEPTH):
        w = a["w_in"][L]
        w = np.concatenate([heads_paired(w[:, :512], 1), w[:, 512:]], axis=1)
        stream.append(tiles_by_column(w))
        wb = np.concatenate([heads_paired(a["w_attn_out"][L], 0), a["w_pool_out"][L], a["w_conv_out"][L]], axis=0)
        stream.append(tiles_by_column(wb))
        stream.append(rows_by_half(a["w_out"][L]))
        if L == 0:
            gu = np.stack([tiles_by_column(a["w_ff_gate"][0]), tiles_by_column(a["w_ff_up"][0])], axis=1)
            stream.append(gu.reshape(-1, P, CH))
            stream.append(rows_by_half(a["w_ff_down"][0]))
    dense = np.concatenate(stream, axis=0)
    gus, dns = [], []
    for e in range(NE):
        gu = np.stack([tiles_by_column(a["w_e_gate"][0, e]), tiles_by_column(a["w_e_up"][0, e])], axis=1)
        gus.append(gu.reshape(-1, P, CH))
        dns.append(tiles_by_column(a["w_e_down"][0, e]))
    vecs = np.zeros((P, DEPTH, V_END), np.float32)
    mix = np.zeros((P, DEPTH, 2, P), np.float32)
    for L in range(DEPTH):
        vecs[:, L, V_QG] = np.tile(a["q_norm_g"][L], 2)
        vecs[:, L, V_KG] = np.tile(a["k_norm_g"][L], 2)
        for name, c, n in (("b_gate", V_BG, 24), ("pool_scale", V_PS, 2), ("b_dw", V_BDW, 2), ("conv_ln_g", V_CG, 2),
                           ("conv_ln_b", V_CB, 2), ("ln1_g", V_L1G, 8), ("ln1_b", V_L1B, 8), ("ln2_g", V_L2G, 8),
                           ("ln2_b", V_L2B, 8)):
            vecs[:, L, c:c + n] = col(a[name][L])
        for ti in range(2):
            vecs[:, L, V_DW + ti * CK:V_DW + (ti + 1) * CK] = a["w_dw"][L][:, ti * P:(ti + 1) * P].T
            for h in range(2):
                s = slice(64 * h, 64 * h + 64)
                mix[s, L, ti, s] = a["w_pool_mix"][L, 2 * ti + h]
    lnrow = np.stack([np.stack([a[f"ln{i}_g"][L], a[f"ln{i}_b"][L]]) for L in range(DEPTH) for i in (1, 2)])
    ins = {
        "x0": a["x_prompt"], "x1": a["x_sample"], "dense_w": dense, "expert_gu": np.concatenate(gus),
        "expert_dn": np.concatenate(dns), "consts": shape_constants(),
        "slots": np.broadcast_to(np.arange(CAP, dtype=np.float32), (P, CAP)), "vecs": vecs, "mix": mix, "lnrow": lnrow,
        "wr": a["w_router"], "br": a["b_router"],
    }
    ins = {k: np.ascontiguousarray(v) for k, v in ins.items()}
    nc = bacc.Bacc("TRN2", target_bir_lowering=False, num_devices=1)
    aps = {k: nc.dram_tensor(k, v.shape, mybir.dt.from_np(v.dtype), kind="ExternalInput").ap()
           for k, v in ins.items()}
    xd = nc.dram_tensor("item_rows", (N_ROWS, D), F32, kind="Internal").ap()
    yd = nc.dram_tensor("item_results", (N_ROWS, D), F32, kind="Internal").ap()
    y0 = nc.dram_tensor("y0", (1, SEQ, D), F32, kind="ExternalOutput").ap()
    y1 = nc.dram_tensor("y1", (1, SEQ, D), F32, kind="ExternalOutput").ap()
    build_trunk(nc, xd=xd, yd=yd, y0=y0, y1=y1, **aps)
    r = run_bass_kernel_spmd(nc, [ins], core_ids=[0])
    return r.results[0]["y0"], r.results[0]["y1"]
```
